# Optimizing a Trainium2 kernel written in Bass

```python
import math
import jax
import jax.numpy as jnp
from jax import lax
import numpy as np

D_MODEL = 1024
BATCH = 1
SEQ = 256
DEPTH = 1
DEC_BATCH = 8
DEC_SEQ = 4
PAST_LEN = 1024
PAGE_SIZE = 128

MLA_HEADS = 8
MLA_NOPE = 64
MLA_ROPE = 32
MLA_V = 64
Q_LORA = 384
KV_LORA = 256
MLA_SCALE = (MLA_NOPE + MLA_ROPE) ** -0.5
DSA_HEADS = 8
DSA_KV_HEADS = 2
DSA_HEAD_DIM = 64
DSA_SCALE = DSA_HEAD_DIM ** -0.5
IDX_HEADS = 8
IDX_DIM = 64
IDX_ROPE = 32
IDX_TOPK_MAX = 256
IDX_W_SCALE = (IDX_HEADS * IDX_DIM) ** -0.5
REL_BUCKETS = 32
REL_MAX_DIST = 128
PEER_HEADS = 8
PEER_NKEYS = 128
PEER_EXPERTS = PEER_NKEYS * PEER_NKEYS
PEER_QDIM = 256
PEER_HALF = PEER_QDIM // 2
PEER_TOPK = 16
PEER_CHUNK = 256

ROPE_THETA = 10000.0
NORM_EPS = 1e-6
Q_BLOCK = 128

SPLITS = (Q_LORA, KV_LORA, MLA_ROPE, DSA_HEADS * DSA_HEAD_DIM, DSA_KV_HEADS * DSA_HEAD_DIM,
          DSA_KV_HEADS * DSA_HEAD_DIM, IDX_HEADS * IDX_DIM, IDX_DIM, IDX_HEADS)
D_IN = sum(SPLITS)
MIX_WIDTH = MLA_HEADS * MLA_V + DSA_HEADS * DSA_HEAD_DIM

kernel_name = 'hybrid_mla_dsa_peer_step'

def rmsnorm(x, g):
    xf = x.astype(jnp.float32)
    y = xf * lax.rsqrt(jnp.mean(xf * xf, axis=-1, keepdims=True) + NORM_EPS)
    return y.astype(x.dtype) * g

def rope(x, pos):
    half = x.shape[-1] // 2
    inv = ROPE_THETA ** (-jnp.arange(half, dtype=jnp.float32) / half)
    ang = pos.astype(jnp.float32)[:, None, None] * inv
    cos, sin = jnp.cos(ang), jnp.sin(ang)
    xf = x.astype(jnp.float32)
    x1, x2 = xf[..., :half], xf[..., half:]
    return jnp.concatenate([x1 * cos - x2 * sin, x2 * cos + x1 * sin], axis=-1).astype(x.dtype)

def rel_bucket(dist):
    max_exact = REL_BUCKETS // 2
    n = jnp.maximum(dist, 0)
    nf = jnp.maximum(n, 1).astype(jnp.float32)
    large = max_exact + (jnp.log(nf / max_exact) / math.log(REL_MAX_DIST / max_exact)
                         * (REL_BUCKETS - max_exact)).astype(jnp.int32)
    large = jnp.minimum(large, REL_BUCKETS - 1)
    return jnp.where(n < max_exact, n, large)

def to_blocks(a):
    b, s = a.shape[:2]
    return a.reshape((b, s // Q_BLOCK, Q_BLOCK) + a.shape[2:]).swapaxes(0, 1)

def from_blocks(a):
    nb, b, qb = a.shape[:3]
    return a.swapaxes(0, 1).reshape((b, nb * qb) + a.shape[3:])

def take_rows(rows, idx):
    return jax.vmap(lambda r, i: r[i])(rows, idx)

def mixer_inputs(xn, pos, w_in, g_q, w_uq, g_kv, w_uk):
    b, s, _ = xn.shape
    cuts = tuple(int(c) for c in np.cumsum(SPLITS)[:-1])
    c_q, c_kv, k_r, q_b, k_b, v_b, q_i, k_i, w_i = jnp.split(xn @ w_in, cuts, axis=-1)
    c_q = rmsnorm(c_q, g_q)
    q = (c_q @ w_uq).reshape(b, s, MLA_HEADS, MLA_NOPE + MLA_ROPE)
    q_lat = jnp.einsum('bshn,chn->bshc', q[..., :MLA_NOPE], w_uk)
    q_rope = rope(q[..., MLA_NOPE:], pos)
    c_kv = rmsnorm(c_kv, g_kv)
    k_rope = rope(k_r[:, :, None, :], pos)[:, :, 0]
    q_b = q_b.reshape(b, s, DSA_KV_HEADS, DSA_HEADS // DSA_KV_HEADS, DSA_HEAD_DIM)
    k_b = k_b.reshape(b, s, DSA_KV_HEADS, DSA_HEAD_DIM)
    v_b = v_b.reshape(b, s, DSA_KV_HEADS, DSA_HEAD_DIM)
    q_i = q_i.reshape(b, s, IDX_HEADS, IDX_DIM)
    q_i = jnp.concatenate([rope(q_i[..., :IDX_ROPE], pos), q_i[..., IDX_ROPE:]], axis=-1)
    k_i = jnp.concatenate([rope(k_i[:, :, None, :IDX_ROPE], pos)[:, :, 0], k_i[..., IDX_ROPE:]], axis=-1)
    w_i = w_i * IDX_W_SCALE
    return q_lat, q_rope, c_kv, k_rope, q_b, k_b, v_b, q_i, k_i, w_i

def mla_logits(q_lat, q_rope, ckv, krope):
    s = jnp.einsum('bthc,bsc->bhts', q_lat, ckv) + jnp.einsum('bthr,bsr->bhts', q_rope, krope)
    return s.astype(jnp.float32) * MLA_SCALE

def mla_out(o_lat, w_uv):
    b, t = o_lat.shape[:2]
    return jnp.einsum('bthc,chv->bthv', o_lat, w_uv).reshape(b, t, MLA_HEADS * MLA_V)

def mla_prompt(q_lat, q_rope, c_kv, k_rope, w_uv):
    b, s = c_kv.shape[:2]
    kpos = jnp.arange(s)

    def block(args):
        ql, qr, qpos = args
        logits = mla_logits(ql, qr, c_kv, k_rope)
        logits = jnp.where((kpos[None, :] <= qpos[:, None])[None, None], logits, -jnp.inf)
        p = jax.nn.softmax(logits, axis=-1).astype(c_kv.dtype)
        return jnp.einsum('bhts,bsc->bthc', p, c_kv)

    qpos = jnp.arange(s).reshape(s // Q_BLOCK, Q_BLOCK)
    o_lat = from_blocks(lax.map(block, (to_blocks(q_lat), to_blocks(q_rope), qpos)))
    return mla_out(o_lat, w_uv)

def mla_sample(q_lat, q_rope, c_kv, k_rope, w_uv, cache_ckv, cache_krope, layer, page_table):
    b, t = c_kv.shape[:2]
    past = page_table.shape[1] * PAGE_SIZE
    ckv_past = cache_ckv[layer, page_table].reshape(b, past, KV_LORA)
    kr_past = cache_krope[layer, page_table].reshape(b, past, MLA_ROPE)
    causal = jnp.arange(t)[None, :] <= jnp.arange(t)[:, None]
    logits = jnp.concatenate(
        [mla_logits(q_lat, q_rope, ckv_past, kr_past),
         jnp.where(causal[None, None], mla_logits(q_lat, q_rope, c_kv, k_rope), -jnp.inf)], axis=-1)
    p = jax.nn.softmax(logits, axis=-1).astype(c_kv.dtype)
    o_lat = (jnp.einsum('bhts,bsc->bthc', p[..., :past], ckv_past)
             + jnp.einsum('bhts,bsc->bthc', p[..., past:], c_kv))
    return mla_out(o_lat, w_uv)

def indexer_scores(q_i, w_i, k_i):
    a = jax.nn.relu(jnp.einsum('bthd,bsd->bths', q_i, k_i).astype(jnp.float32))
    return jnp.einsum('bth,bths->bts', w_i.astype(jnp.float32), a)

def dsa_attend(q, k_sel, v_sel, s_sel, qpos, rel_bias):
    b, t, g, r, d = q.shape
    dist = qpos[None, :, None] - s_sel
    bias = rel_bias[rel_bucket(dist)].astype(jnp.float32)
    bias = bias.transpose(0, 1, 3, 2).reshape(b, t, g, r, -1)
    logits = jnp.einsum('btgrd,btkgd->btgrk', q, k_sel).astype(jnp.float32) * DSA_SCALE + bias
    logits = jnp.where((dist >= 0)[:, :, None, None, :], logits, -jnp.inf)
    p = jax.nn.softmax(logits, axis=-1).astype(v_sel.dtype)
    return jnp.einsum('btgrk,btkgd->btgrd', p, v_sel).reshape(b, t, g * r * d)

def dsa_prompt(q_b, k_b, v_b, q_i, k_i, w_i, rel_bias):
    b, s = k_b.shape[:2]
    topk = min(IDX_TOPK_MAX, s // 4)
    kpos = jnp.arange(s)

    def block(args):
        qb, qib, wib, qpos = args
        sc = indexer_scores(qib, wib, k_i)
        sc = jnp.where((kpos[None, :] <= qpos[:, None])[None], sc, -jnp.inf)
        _, idx = lax.top_k(sc, topk)
        return dsa_attend(qb, take_rows(k_b, idx), take_rows(v_b, idx), idx, qpos, rel_bias)

    qpos = jnp.arange(s).reshape(s // Q_BLOCK, Q_BLOCK)
    return from_blocks(lax.map(block, (to_blocks(q_b), to_blocks(q_i), to_blocks(w_i), qpos)))

def gather_rows(pool, layer, new_rows, page_table, idx):
    b, t, k = idx.shape
    past = page_table.shape[1] * PAGE_SIZE
    ip = jnp.minimum(idx, past - 1)
    phys = jnp.take_along_axis(page_table, (ip // PAGE_SIZE).reshape(b, t * k), axis=1).reshape(b, t, k)
    from_pool = pool[layer, phys, ip % PAGE_SIZE]
    from_new = take_rows(new_rows, jnp.clip(idx - past, 0, new_rows.shape[1] - 1))
    is_past = (idx < past).reshape(idx.shape + (1,) * (from_pool.ndim - 3))
    return jnp.where(is_past, from_pool, from_new)

def dsa_sample(q_b, k_b, v_b, q_i, k_i, w_i, cache_k, cache_v, cache_kidx, layer, page_table, qpos, rel_bias):
    b, t = k_b.shape[:2]
    past = page_table.shape[1] * PAGE_SIZE
    topk = min(IDX_TOPK_MAX, (past + t) // 4)
    kidx_past = cache_kidx[layer, page_table].reshape(b, past, IDX_DIM)
    causal = jnp.arange(t)[None, :] <= jnp.arange(t)[:, None]
    sc = jnp.concatenate([indexer_scores(q_i, w_i, kidx_past),
                          jnp.where(causal[None], indexer_scores(q_i, w_i, k_i), -jnp.inf)], axis=-1)
    _, idx = lax.top_k(sc, topk)
    k_sel = gather_rows(cache_k, layer, k_b, page_table, idx)
    v_sel = gather_rows(cache_v, layer, v_b, page_table, idx)
    return dsa_attend(q_b, k_sel, v_sel, idx, qpos, rel_bias)

def peer_ffn(x, w_pq, sub_keys, u_emb, v_emb):
    n, d = x.shape
    xp = jnp.pad(x, ((0, -n % PEER_CHUNK), (0, 0))).reshape(-1, PEER_CHUNK, d)

    def chunk(xc):
        c = xc.shape[0]
        q = (xc @ w_pq).reshape(c, PEER_HEADS, 2, PEER_HALF)
        s = jnp.einsum('chpd,hpkd->chpk', q, sub_keys).astype(jnp.float32)
        sv, si = lax.top_k(s, PEER_TOPK)
        cand = (sv[:, :, 0, :, None] + sv[:, :, 1, None, :]).reshape(c, PEER_HEADS, -1)
        cid = (si[:, :, 0, :, None] * PEER_NKEYS + si[:, :, 1, None, :]).reshape(c, PEER_HEADS, -1)
        cv, ci = lax.top_k(cand, PEER_TOPK)
        eid = jnp.take_along_axis(cid, ci, axis=-1)
        gate = jax.nn.softmax(cv, axis=-1)
        act = jax.nn.gelu(jnp.einsum('chkd,cd->chk', u_emb[eid], xc), approximate=False)
        return jnp.einsum('chk,chkd->cd', (gate * act.astype(jnp.float32)).astype(xc.dtype), v_emb[eid])

    return lax.map(chunk, xp).reshape(-1, d)[:n]

def peer_block(h, g_ffn, w_pq, sub_keys, u_emb, v_emb):
    xn = rmsnorm(h, g_ffn)
    return h + peer_ffn(xn.reshape(-1, h.shape[-1]), w_pq, sub_keys, u_emb, v_emb).reshape(h.shape)

def setup_inputs(seed: int = 0) -> dict:
    key = jax.random.key(seed)
    ks = jax.random.split(key, 24)
    f32 = jnp.float32
    n_pages = PAST_LEN // PAGE_SIZE
    n_used = DEC_BATCH * n_pages
    n_pool = n_used + n_used // 4

    def nrm(k, shape, scale=1.0):
        return jax.random.normal(k, shape, f32) * scale

    def gain(k, shape):
        return 1.0 + 0.02 * jax.random.normal(k, shape, f32)

    page_table = jax.random.permutation(ks[7], n_pool)[:n_used].reshape(DEC_BATCH, n_pages).astype(jnp.int32)
    return {
        'x_prompt': nrm(ks[0], (BATCH, SEQ, D_MODEL)),
        'x_sample': nrm(ks[1], (DEC_BATCH, DEC_SEQ, D_MODEL)),
        'cache_ckv': nrm(ks[2], (DEPTH, n_pool, PAGE_SIZE, KV_LORA)),
        'cache_krope': nrm(ks[3], (DEPTH, n_pool, PAGE_SIZE, MLA_ROPE)),
        'cache_k': nrm(ks[4], (DEPTH, n_pool, PAGE_SIZE, DSA_KV_HEADS, DSA_HEAD_DIM)),
        'cache_v': nrm(ks[5], (DEPTH, n_pool, PAGE_SIZE, DSA_KV_HEADS, DSA_HEAD_DIM)),
        'cache_kidx': nrm(ks[6], (DEPTH, n_pool, PAGE_SIZE, IDX_DIM)),
        'page_table': page_table,
        'rel_bias': nrm(ks[8], (REL_BUCKETS, DSA_HEADS), 0.5),
        'g_attn': gain(ks[9], (DEPTH, D_MODEL)),
        'w_in': nrm(ks[10], (DEPTH, D_MODEL, D_IN), D_MODEL ** -0.5),
        'g_q': gain(ks[11], (DEPTH, Q_LORA)),
        'w_uq': nrm(ks[12], (DEPTH, Q_LORA, MLA_HEADS * (MLA_NOPE + MLA_ROPE)), Q_LORA ** -0.5),
        'g_kv': gain(ks[13], (DEPTH, KV_LORA)),
        'w_uk': nrm(ks[14], (DEPTH, KV_LORA, MLA_HEADS, MLA_NOPE), KV_LORA ** -0.5),
        'w_uv': nrm(ks[15], (DEPTH, KV_LORA, MLA_HEADS, MLA_V), KV_LORA ** -0.5),
        'w_out': nrm(ks[16], (DEPTH, MIX_WIDTH, D_MODEL), MIX_WIDTH ** -0.5),
        'g_ffn': gain(ks[17], (DEPTH, D_MODEL)),
        'w_pq': nrm(ks[18], (DEPTH, D_MODEL, PEER_HEADS * PEER_QDIM), D_MODEL ** -0.5),
        'peer_keys': nrm(ks[19], (DEPTH, PEER_HEADS, 2, PEER_NKEYS, PEER_HALF), PEER_HALF ** -0.5),
        'peer_u': nrm(ks[20], (DEPTH, PEER_EXPERTS, D_MODEL), D_MODEL ** -0.5),
        'peer_v': nrm(ks[21], (DEPTH, PEER_EXPERTS, D_MODEL), PEER_HEADS ** -0.5),
        'g_final': gain(ks[22], (D_MODEL,)),
    }

def reference(x_prompt, x_sample, cache_ckv, cache_krope, cache_k, cache_v, cache_kidx, page_table,
              rel_bias, g_attn, w_in, g_q, w_uq, g_kv, w_uk, w_uv, w_out, g_ffn, w_pq, peer_keys,
              peer_u, peer_v, g_final):
    hp, hs = x_prompt, x_sample
    pos_p = jnp.arange(x_prompt.shape[1])
    pos_s = page_table.shape[1] * PAGE_SIZE + jnp.arange(x_sample.shape[1])
    rows_p = [[], [], [], [], []]
    rows_s = [[], [], [], [], []]
    for l in range(DEPTH):
        q_lat, q_rope, c_kv, k_rope, q_b, k_b, v_b, q_i, k_i, w_i = mixer_inputs(
            rmsnorm(hp, g_attn[l]), pos_p, w_in[l], g_q[l], w_uq[l], g_kv[l], w_uk[l])
        mix = jnp.concatenate([mla_prompt(q_lat, q_rope, c_kv, k_rope, w_uv[l]),
                               dsa_prompt(q_b, k_b, v_b, q_i, k_i, w_i, rel_bias)], axis=-1)
        hp = hp + mix @ w_out[l]
        hp = peer_block(hp, g_ffn[l], w_pq[l], peer_keys[l], peer_u[l], peer_v[l])
        for lst, a in zip(rows_p, (c_kv, k_rope, k_b, v_b, k_i)):
            lst.append(a)
        q_lat, q_rope, c_kv, k_rope, q_b, k_b, v_b, q_i, k_i, w_i = mixer_inputs(
            rmsnorm(hs, g_attn[l]), pos_s, w_in[l], g_q[l], w_uq[l], g_kv[l], w_uk[l])
        mix = jnp.concatenate([
            mla_sample(q_lat, q_rope, c_kv, k_rope, w_uv[l], cache_ckv, cache_krope, l, page_table),
            dsa_sample(q_b, k_b, v_b, q_i, k_i, w_i, cache_k, cache_v, cache_kidx, l, page_table,
                       pos_s, rel_bias)], axis=-1)
        hs = hs + mix @ w_out[l]
        hs = peer_block(hs, g_ffn[l], w_pq[l], peer_keys[l], peer_u[l], peer_v[l])
        for lst, a in zip(rows_s, (c_kv, k_rope, k_b, v_b, k_i)):
            lst.append(a)
    y_prompt = rmsnorm(hp, g_final)
    y_sample = rmsnorm(hs, g_final)
    new_ckv_p, new_krope_p, new_k_p, new_v_p, new_kidx_p = [jnp.stack(r, axis=0) for r in rows_p]
    new_ckv_s, new_krope_s, new_k_s, new_v_s, new_kidx_s = [jnp.stack(r, axis=0) for r in rows_s]
    return (y_prompt, y_sample, new_ckv_p, new_krope_p, new_k_p, new_v_p, new_kidx_p,
            new_ckv_s, new_krope_s, new_k_s, new_v_s, new_kidx_s)


_drawn_inputs = setup_inputs


def setup_inputs(seed=0):
    import zlib

    import numpy as np

    out = dict(_drawn_inputs(seed))
    spreads = {}
    factors = {'g_q': 5.995, 'g_kv': 2.679, 'g_final': 7.918, 'g_ffn': 2.861}
    for name, (base, spread) in spreads.items():
        noise = np.random.default_rng([zlib.crc32(name.encode()), seed]).standard_normal(out[name].shape)
        drawn = base * np.exp(spread * noise) if base else spread * noise
        out[name] = jnp.asarray(drawn.astype(out[name].dtype))
    for name, factor in factors.items():
        out[name] = (out[name] * factor).astype(out[name].dtype)
    return out
```

```python
import math
from contextlib import ExitStack

import numpy as np
import concourse.bass as bass
from concourse import mybir

F32 = mybir.dt.float32
U32 = mybir.dt.uint32
I32 = mybir.dt.int32
ALU = mybir.AluOpType
ACT = mybir.ActivationFunctionType
AX = mybir.AxisListType

DM, SEQ, NB, NT, PAST, PAGE = 1024, 256, 8, 4, 1024, 128
NPG = PAST // PAGE
NH, NOPE, ROPE, VD = 8, 64, 32, 64
QL, KVL = 384, 256
KG, HD = 2, 64
HR = NH // KG
IDX = 64
QKD = IDX + ROPE
EPS = 1e-6
MLA_SCALE = (NOPE + ROPE) ** -0.5
DSA_SCALE = HD ** -0.5
IDX_W = (NH * IDX) ** -0.5
TOPK_P, TOPK_S = 64, 256
REL_B = 32
KEYS, EXPERTS, PTOP = 128, 128 * 128, 16
P = [128, 128, NB * NT]
ROW0 = [0, 128, 256]
GROUPS = [[0], [1, 2]]
IN_GROUP = [0, 0, 1]
SPL = [QL, KVL, ROPE, NH * HD, KG * HD, KG * HD, NH * IDX, IDX, NH]
OFF = [sum(SPL[:i]) for i in range(len(SPL))]
O_CQ, O_CKV, O_KR, O_QB, O_KB, O_VB, O_QI, O_KI, O_WI = OFF
DIN = sum(SPL)
ZC = [512, 512, 512, DIN - 1536]
SK = PAST + NB * NT
UC = [(0, 512), (512, 512), (1024, NB * NT)]
NEG = -1e30
TAKEN = -3e38
ARENA = 29700
GU = 1156
WD = 383
WS = 1031

CONSTS_IN, SETUP_IN = 16 * 17, 16 * 4
MEETINGS = 9
NRING = 6
NW = 2
G, D = 2, 4
NR = G * D
SLOTS = [128, 128, 32]


def free(ap, *dims):
    return bass.AP(ap.tensor, ap.offset, [list(ap.ap[0])] + [list(d) for d in dims])


def build(nc, inp, cst, out, scr_d, scr_s):
    ctx = ExitStack()
    with ctx:
        def sb(name, shape, dt=F32):
            return ctx.enter_context(nc.sbuf_tensor(name, shape, dt))

        def sem(name):
            return ctx.enter_context(nc.semaphore(name))

        ident = sb("ident", [128, 128])
        tri = sb("tri", [128, 256])
        sel_sample = sb("sel_sample", [128, 128])
        iota16 = sb("iota16", [128, 16])
        ropet = sb("ropet", [128, 3, 64])
        g_attn = sb("g_attn_sb", [128, DM])
        g_ffn = sb("g_ffn_sb", [128, DM])
        g_fin = g_attn
        g_q = sb("g_q_sb", [128, QL])
        g_kv = sb("g_kv_sb", [128, KVL])
        newmask = sb("newmask", [32, NB, 32])
        newmask_i = sb("newmask_i", [32, 32])
        rep = sb("rep", [32, NB, 32])
        rowsum = sb("rowsum", [32, NB, 32])
        ones = sb("ones", [32, 1])
        page_sb = sb("page_sb", [1, NB * NPG], I32)
        w_uq = sb("w_uq_sb", [128, 3, NH * QKD])
        uk_t = sb("uk_t", [128, HR, KVL])
        w_uv = sb("w_uv_sb", [128, 2, NH * VD])
        keys_t = sb("keys_t", [128, 16, KEYS])
        bias_d = sb("bias_d", [128, NH, 256])
        bias_s = sb("bias_s", [32, SK])
        x = [sb(f"x{t}", [128, DM]) for t in range(3)]
        xn2 = [sb(f"xn2_{t}", [128, DM]) for t in range(3)]
        eid = [sb(f"eid{t}", [128, SLOTS[t]], U32) for t in range(3)]
        gate = [sb(f"gate{t}", [128, SLOTS[t]]) for t in range(3)]
        ckv_nat = sb("ckv_nat", [128, 3, KVL])
        v_nat = sb("v_nat", [128, 3, 128])
        ckv_t = sb("ckv_t", [128, 2, 288])
        kk_t = sb("kk_t", [QKD, 288])
        kb_t = sb("kb_t", [128, 288])
        small = sb("small", [128, 256])
        arena = sb("arena", [128, ARENA])
        used = {"front": 0, "peer": 0}

        def region(name, kind, parts, *shape):
            n = int(np.prod(shape))
            a = arena[0:parts, used[kind]:used[kind] + n]
            used[kind] += n
            assert used[kind] <= ARENA, (name, used[kind])
            if len(shape) == 1:
                return a
            names = "abc"[:len(shape)]
            return a.rearrange(f"p ({' '.join(names)}) -> p {' '.join(names)}", **dict(zip(names[1:], shape[1:])))

        wring = [region(f"wring{i}", "front", 128, 8, 512) for i in range(NW)]
        z = [region(f"z{i}", "front", 128, DIN) for i in range(2)]
        xt = [region(f"xt{i}", "front", 128, 8, P[2 * i]) for i in range(2)]
        mix_t = [region(f"mix_t{i}", "front", 128, 8, P[2 * i]) for i in range(2)]
        ql_t = region("ql_t", "front", 128, 2, NH, 128)
        o_t = region("o_t", "front", 128, 2, NH, 128)
        qq_t = region("qq_t", "front", QKD, NH, 128)
        qn_t = region("qn_t", "front", 128, HR, 128)
        qb_t = region("qb_t", "front", 128, HR, 128)
        cq_t = region("cq_t", "front", 128, 3, 128)
        qp_t = [qb_t, qn_t]
        ql_s = ql_t[:, :, 0:2, :].rearrange("p c h n -> p c (h n)").rearrange("p c (b q) -> p c b q", q=32)
        qq_s = qq_t[:, 0:2, :].rearrange("p h n -> p (h n)").rearrange("p (b q) -> p b q", q=32)
        shared = used["front"]
        s_b = [region(f"s{i}", "front", 128, 512) for i in range(2)]
        p_t = [region(f"p_t{i}", "front", 128, 512) for i in range(2)]
        relu = [region(f"relu{i}", "front", 128, 512) for i in range(2)]
        bm = region("bm", "front", 128, NH, 256)
        iscore = region("iscore", "front", 128, 256)
        iwork = region("iwork", "front", 128, 256)
        q_nope = region("q_nope", "front", 128, NH * NOPE)
        q_rope = region("q_rope", "front", 128, NH * ROPE)
        qb_pairs = relu[0]
        cqn = region("cqn", "front", 128, QL)
        kk = region("kk", "front", 128, QKD)
        rope_a = region("rope_a", "front", 128, NH, 32)
        rope_b = region("rope_b", "front", 128, NH, 32)
        qq = region("qq", "front", 128, NH, QKD)
        top_front = used["front"]
        natc = [wring[i][:, 0:4, :].rearrange("p a (b c) -> p (a b) c", c=256) for i in range(2)]
        natk = [wring[i][:, 4:6, :].rearrange("p a (b c) -> p (a b) c", c=128) for i in range(2)]
        natk96 = [k[:, :, 0:QKD] for k in natk]
        natv = [wring[i][:, 6:8, :].rearrange("p a (b c) -> p (a b) c", c=128) for i in range(2)]
        used["front"] = shared
        ckp_t = region("ckp_t", "front", 128, 2, PAST)
        kkp_t = region("kkp_t", "front", 128, PAST)
        s_s = region("s_s", "front", 32, SK)
        a_s = region("a_s", "front", 32, SK)
        pt_s = region("pt_s", "front", 128, 9, 32)
        i_s = region("i_s", "front", 32, SK)
        wrk_s = region("wrk_s", "front", 32, SK)
        qblk = region("qblk", "front", 128, NB, 32)
        wexp = region("wexp", "front", 32, NB, 32)
        wcol = region("wcol", "front", 32, NB)
        used["front"] = shared
        sc = region("sc", "front", 128, 4, KEYS)
        sv = [region(f"sv{i}", "front", 128, 16, PTOP) for i in range(2)]
        si = region("si", "front", 128, 16, PTOP)
        si_u = [region(f"si_u{i}", "front", 128, 16, PTOP).bitcast(U32) for i in range(2)]
        cand = region("cand", "front", 128, NH, 256)
        cv = region("cv", "front", 128, NH, PTOP)
        ci = region("ci", "front", 128, NH, PTOP).bitcast(U32)
        ca = region("ca", "front", 128, NH, PTOP).bitcast(U32)
        hot = region("hot", "front", 128, NH * PTOP, 16)
        ea = region("ea", "front", 128, NH * PTOP)
        eb = region("eb", "front", 128, NH * PTOP)
        eu = region("eu", "front", 128, NH * PTOP).bitcast(U32)
        gt = region("gt", "front", 128, NH, PTOP)
        used["front"] = shared
        relb = region("relb", "front", 32, NH)
        relb_x = region("relb_x", "front", 32, NH, 128)
        relb_s = region("relb_s", "front", 32, NH, NT)
        hot_u = region("hot_u", "front", 32, GU)
        gd = region("gd", "front", 128, NH, WD)
        gs = region("gs", "front", 32, WS)
        keys_nat = o_t.rearrange("p c h n -> p (c h) n")
        uk_nat = ql_t[:, 0, :, :].rearrange("p (c r) n -> p c (r n)", c=2)

        u_ring = [region(f"u{i}", "peer", 128, DM) for i in range(NR)]
        v_ring = [region(f"v{i}", "peer", 128, DM) for i in range(NR)]
        d_ring = [region(f"diag{i}", "peer", 128, 128) for i in range(NR)]
        stage = sb("stage", [128, D, G], U32)
        dots = sb("dots", [128, D, G])
        wts = sb("wts", [128, D, G])

        acc = ctx.enter_context(nc.psum_tensor("acc", [128, DM], F32))
        banks = [ctx.enter_context(nc.psum_tensor(f"bank{i}", [128, 512], F32)) for i in range(NRING)]
        bank_full = [sem(f"bank{i}_full") for i in range(NRING)]
        bank_free = [sem(f"bank{i}_free") for i in range(NRING)]
        turn = {}

        def take(pe, name):
            n = turn[name] = len(turn)
            if n >= NRING:
                pe.wait_ge(bank_free[n % NRING], n // NRING)
            return banks[n % NRING]

        def full(ins, name):
            ins.then_inc(bank_full[turn[name] % NRING], 1)

        def ready(eng, name):
            n = turn[name]
            eng.wait_ge(bank_full[n % NRING], n // NRING + 1)
            return banks[n % NRING]

        def drained(ins, name):
            ins.then_inc(bank_free[turn[name] % NRING], 1)

        def read_done(eng, name):
            n = turn[name]
            eng.wait_ge(bank_free[n % NRING], n // NRING + 1)

        class Signal:

            def __init__(self, name, steps, unit=1):
                self.sem, self.unit, self.sent = sem(name), unit, 0
                self.at = {k: i + 1 for i, k in enumerate(steps)}

            def send(self, ins, step):
                self.sent += 1
                assert self.at[step] == self.sent, (self.at, step)
                ins.then_inc(self.sem, self.unit)

            def wait(self, eng, step):
                eng.wait_ge(self.sem, self.at[step] * self.unit)

        tiles = [0, 1, 2]
        consts_in = sem("consts_in")
        setup_in = sem("setup_in")
        small_w_in = sem("small_w_in")
        x_in = [sem(f"x{t}_in") for t in tiles]
        x2_zero = sem("x2_zero")
        gfin_in = sem("gfin_in")
        w_in_slot = [sem(f"w_slot{i}_in") for i in range(NW)]
        CHUNKS = [(g, w, c) for g in range(2) for w, n in (("in", 4), ("out", 2), ("pq", 4)) for c in range(n)]
        W_DMAS = {"in": 1, "out": 3, "pq": 1}
        page_ids_in = sem("page_ids_in")
        lat_in = [sem(f"latent_pages{i}_in") for i in range(2)]
        kv_in = [sem(f"kv_pages{i}_in") for i in range(2)]
        lat_used = Signal("latent_pages_used", range(NB))
        kv_used = Signal("kv_pages_used", range(NB))
        scr_d_out, scr_s_out, bias_in = sem("scratch_d_out"), sem("scratch_s_out"), sem("bias_in")
        stored = sem("stored")
        stored_z = sem("stored_z")
        met = sem("met")
        xn_ready = Signal("xn_ready", tiles)
        relb_ready = Signal("relb_ready", [0])
        post_ready = Signal("post_ready", tiles)
        qrope_ready = Signal("qrope_ready", tiles)
        HG = [NH * P[1] * (t + 1) // 512 for t in (0, 1)]
        probs_ready = Signal("probs_ready", [(k, t, g) for t in (0, 1) for k in "md" for g in range(HG[t])]
                             + [("m", b) for b in range(NB)] + [("d", b) for b in range(NB)])
        logits_sb = Signal("logits_sb", list(probs_ready.at))
        exps_ready = Signal("exps_ready", list(probs_ready.at))
        relu_used = Signal("relu_used", [(t, g) for t in (0, 1) for g in range(HG[t])])
        wexp_ready = Signal("wexp_ready", [0])
        sel_ready = Signal("sel_ready", [0])
        xn2_ready = Signal("xn2_ready", tiles)
        ROOTS = [r for g in range(2) for r in [("x", t) for t in GROUPS[g]] + [("z", t) for t in GROUPS[g]]
                 + [("h", t) for t in GROUPS[g]]] + [("y", t) for t in tiles]
        square_ready = Signal("mean_square_ready", ROOTS)
        root_ready = Signal("root_ready", ROOTS)
        gate_sub = Signal("gate_sub", tiles)
        gate_exp = Signal("gate_exp", tiles)
        slots_ready = Signal("slots_ready", tiles)
        chain_v, chain_a, chain_p = sem("vector_chain"), sem("scalar_chain"), sem("gpsimd_chain")
        links = {"v": 0, "a": 0, "p": 0}
        meetings = {}

        def link(eng, ins):
            k, s = {id(nc.vector): ("v", chain_v), id(nc.scalar): ("a", chain_a),
                    id(nc.gpsimd): ("p", chain_p)}[id(eng)]
            links[k] += 1
            ins.then_inc(s, 1)
            eng.wait_ge(s, links[k])

        def chunk_count(n):
            return 16 * sum(W_DMAS[CHUNKS[m][1]] for m in range(n % NW, n + 1, NW))

        def meet(eng, key):
            meetings[id(eng)] = meetings.get(id(eng), 0) + 1
            eng.drain().then_inc(met, 1)
            eng.wait_ge(met, 3 * meetings[id(eng)])

        u_in = [sem(f"u{i}_in") for i in range(NR)]
        v_in = [sem(f"v{i}_in") for i in range(NR)]
        staged = sem("slots_staged")
        gate_p, gate_a = sem("gpsimd_passed"), sem("scalar_passed")
        dots_done, gelu_done, wts_done = sem("dots_done"), sem("gelu_done"), sem("weights_done")
        diag_done, sums_done = sem("diagonals_done"), sem("sums_done")
        acc_read = Signal("acc_read", tiles)
        y_ready = Signal("y_ready", tiles)
        GRAN = [SLOTS[t] // G for t in tiles]
        BASE = [sum(GRAN[:t]) for t in tiles]

        block = ctx.enter_context(nc.Block())

        T = nc.tensor
        V = nc.vector
        A = nc.scalar

        def mm(o, l, r, start=True, stop=True):
            return T.matmul(o, lhsT=l, rhs=r, start=start, stop=stop, skip_group_check=True)

        def tr(o, i):
            return T.transpose(o, i, ident[0:i.shape[0], 0:i.shape[0]])

        def experts_pe(pe):
            for t in tiles:
                if t:
                    acc_read.wait(pe, t - 1)
                mm(acc[:, 0:512], ident[:, :], x[t][:, 0:512], True, False)
                i = mm(acc[:, 512:1024], ident[:, :], x[t][:, 512:1024], True, False)
                if t == 0:
                    i.then_inc(sums_done, D)
                with pe.Fori(0, GRAN[t] // D) as it:
                    for d in range(D):
                        n = BASE[t] + it * D + d
                        pe.wait_ge(diag_done, n + 1)
                        for j in range(G):
                            k = d * G + j
                            pe.wait_ge(v_in[k], (it + (BASE[t] // D + 1)) * 16)
                            for c in range(2):
                                i = mm(acc[:, c * 512:c * 512 + 512], d_ring[k][:, :],
                                       v_ring[k][:, c * 512:c * 512 + 512], False, False)
                        i.then_inc(sums_done, 1)

        @block.tensor
        def _(pe):
            pe.wait_ge(consts_in, CONSTS_IN)
            pe.wait_ge(setup_in, SETUP_IN)
            for c in range(4):
                b = take(pe, ("keys", c))
                for j in range(4):
                    i = tr(b[:, j * 128:(j + 1) * 128], keys_nat[:, 4 * c + j, :])
                full(i, ("keys", c))
            for c in range(2):
                b = take(pe, ("uk", c))
                for r in range(HR):
                    i = tr(b[:, r * 128:(r + 1) * 128], uk_nat[:, c, r * 128:(r + 1) * 128])
                full(i, ("uk", c))
            relb_ready.wait(pe, 0)
            for h in range(NH):
                b = take(pe, ("bias_d", h))
                full(mm(b[:, 0:WD], relb_x[:, h, :], hot_u[:, GU - 384:GU - 384 + WD]), ("bias_d", h))
            for c in range(3):
                w = min(512, WS - 512 * c)
                b = take(pe, ("bias_s", c))
                full(mm(b[0:32, 0:w], relb_s[:, :, :].rearrange("p h t -> p (h t)"), hot_u[:, c * 512:c * 512 + w]),
                     ("bias_s", c))

            def transpose_x(t, what):
                for c in range(2):
                    b = take(pe, (what, t, c))
                    src = z[IN_GROUP[t]] if what == "x" else xn2[t]
                    for j in range(4):
                        k = 4 * c + j
                        i = tr(b[:, j * P[t]:(j + 1) * P[t]], src[0:P[t], k * 128:(k + 1) * 128])
                    full(i, (what, t, c))

            def chunk_wait(key):
                n = CHUNKS.index(key)
                pe.wait_ge(w_in_slot[n % NW], chunk_count(n))
                return wring[n % NW]

            def heads_part(t):
                n, r0 = P[t], ROW0[t]
                post_ready.wait(pe, t)
                b = take(pe, ("cq", t))
                for j in range(3):
                    i = tr(b[:, j * n:(j + 1) * n], cqn[0:n, j * 128:(j + 1) * 128])
                full(i, ("cq", t))
                b = take(pe, ("kv", t))
                for j in range(2):
                    tr(b[:, j * 128:j * 128 + n], ckv_nat[0:n, t, j * 128:(j + 1) * 128])
                tr(b[0:QKD, 256:256 + n], kk[0:n, :])
                full(tr(b[:, 384:384 + n], z[IN_GROUP[t]][0:n, O_KB:O_KB + 128]), ("kv", t))
                b = take(pe, ("qb", t))
                for r in range(HR):
                    i = tr(b[:, r * n:(r + 1) * n], qb_pairs[0:n, r * 128:(r + 1) * 128])
                full(i, ("qb", t))
                read_done(pe, ("cq", t))
                for c in range(2):
                    b = take(pe, ("q", t, c))
                    for k in range(3):
                        i = mm(b[0:n, 0:384], cq_t[:, k, 0:n], w_uq[:, k, c * 384:(c + 1) * 384], k == 0, k == 2)
                    full(i, ("q", t, c))
                qrope_ready.wait(pe, t)
                b = take(pe, ("qn", t))
                for r in range(HR):
                    i = tr(b[:, r * n:(r + 1) * n], q_nope[0:n, r * 128:(r + 1) * 128])
                full(i, ("qn", t))
                for c in range(2):
                    b = take(pe, ("qq", t, c))
                    for j in range(4):
                        i = tr(b[0:QKD, j * n:(j + 1) * n], qq[0:n, 4 * c + j, :])
                    full(i, ("qq", t, c))
                read_done(pe, ("qn", t))
                for u in range(4):
                    b = take(pe, ("ql", t, u))
                    q, j = u // 2, u % 2
                    for m in range(2):
                        for c in range(2):
                            i = mm(b[:, (2 * c + m) * n:(2 * c + m + 1) * n],
                                   uk_t[j * 64:j * 64 + 64, 2 * q + m, c * 128:(c + 1) * 128],
                                   qn_t[j * 64:j * 64 + 64, 2 * q + m, 0:n])
                    full(i, ("ql", t, u))

            def values_up(t):
                n = P[t]
                b = take(pe, ("uv", t))
                for h in range(NH):
                    for c in range(2):
                        i = mm(b[(h % 2) * 64:(h % 2) * 64 + 64, (h // 2) * n:(h // 2 + 1) * n],
                               w_uv[:, c, h * VD:(h + 1) * VD], o_t[:, c, h, 0:n], c == 0, c == 1)
                full(i, ("uv", t))

            def prompt(t):
                nk = 128 * (t + 1)
                hp = 512 // nk
                read_done(pe, ("qq", t, 1))
                read_done(pe, ("kv", t))
                for g in range(HG[t]):
                    b = take(pe, ("idx", t, g))
                    for j in range(hp):
                        i = mm(b[:, j * nk:(j + 1) * nk], qq_t[0:IDX, g * hp + j, :], kk_t[0:IDX, 0:nk])
                    full(i, ("idx", t, g))
                read_done(pe, ("ql", t, 3))

                def logits(kind, g):
                    b = take(pe, (kind, t, g))
                    for j in range(hp):
                        h, o = g * hp + j, b[:, j * nk:(j + 1) * nk]
                        if kind == "m":
                            mm(o, ql_t[:, 0, h, :], ckv_t[:, 0, 0:nk], True, False)
                            mm(o, ql_t[:, 1, h, :], ckv_t[:, 1, 0:nk], False, False)
                            i = mm(o, qq_t[IDX:QKD, h, :], kk_t[IDX:QKD, 0:nk], False, True)
                        else:
                            g2 = h // HR
                            i = mm(o, qb_t[g2 * 64:g2 * 64 + 64, h % HR, :], kb_t[g2 * 64:g2 * 64 + 64, 0:nk])
                    full(i, (kind, t, g))

                def probs(kind, g):
                    probs_ready.wait(pe, (kind, t, g))
                    b = take(pe, (kind + "pt", t, g))
                    for j in range(4):
                        i = tr(b[:, j * 128:(j + 1) * 128], s_b[g % 2][:, j * 128:(j + 1) * 128])
                    full(i, (kind + "pt", t, g))

                for g in range(HG[t] + 1):
                    if g < HG[t]:
                        logits("m", g)
                    if g:
                        probs("m", g - 1)
                        read_done(pe, ("mpt", t, g - 1))
                        for c in range(2):
                            b = take(pe, ("ol", t, g - 1, c))
                            for j in range(hp):
                                for k in range(t + 1):
                                    i = mm(b[:, j * 128:(j + 1) * 128], ckv_nat[:, k, c * 128:(c + 1) * 128],
                                           p_t[(g - 1) % 2][:, (j * (t + 1) + k) * 128:(j * (t + 1) + k + 1) * 128],
                                           k == 0, k == t)
                            full(i, ("ol", t, g - 1, c))
                read_done(pe, ("ol", t, HG[t] - 1, 1))
                values_up(t)
                for g in range(HG[t] + 1):
                    if g < HG[t]:
                        logits("d", g)
                    if g:
                        probs("d", g - 1)
                        read_done(pe, ("dpt", t, g - 1))
                        b = take(pe, ("od", t, g - 1))
                        for j in range(hp):
                            h = (g - 1) * hp + j
                            for k in range(t + 1):
                                i = mm(b[(h // HR) * 64:(h // HR) * 64 + 64, j * 128:(j + 1) * 128],
                                       v_nat[:, k, (h // HR) * 64:(h // HR) * 64 + 64],
                                       p_t[(g - 1) % 2][:, (j * (t + 1) + k) * 128:(j * (t + 1) + k + 1) * 128],
                                       k == 0, k == t)
                        full(i, ("od", t, g - 1))

            def sample():
                r0 = ROW0[2]
                new = slice(r0, r0 + 32)

                def transposed(kind, b):
                    if kind == "m":
                        pe.wait_ge(lat_in[b % 2], 48 * (b // 2 + 1) * NPG)
                        for p in range(0, NPG, 2):
                            k = take(pe, ("pc", b, p))
                            for c in range(2):
                                for q in range(2):
                                    i = tr(k[:, (2 * c + q) * 128:(2 * c + q + 1) * 128],
                                           natc[b % 2][:, p + q, c * 128:(c + 1) * 128])
                            full(i, ("pc", b, p))
                        for c in range(2):
                            k = take(pe, ("pk", b, c))
                            for q in range(4):
                                i = tr(k[0:QKD, q * 128:(q + 1) * 128], natk96[b % 2][:, 4 * c + q, :])
                            full(i, ("pk", b, c))
                    else:
                        pe.wait_ge(kv_in[b % 2], 32 * (b // 2 + 1) * NPG)
                        for c in range(2):
                            k = take(pe, ("pb", b, c))
                            for q in range(4):
                                i = tr(k[:, q * 128:(q + 1) * 128], natk[b % 2][:, 4 * c + q, :])
                            full(i, ("pb", b, c))

                def attend(kind, b):
                    probs_ready.wait(pe, (kind, b))
                    k = take(pe, (kind + "spt", b))
                    s = s_s
                    for p in range(NPG):
                        tr(k[:, p * 32:(p + 1) * 32], s[:, p * 128:(p + 1) * 128])
                    full(tr(k[0:32, 256:288], s[:, PAST:SK]), (kind + "spt", b))
                    read_done(pe, (kind + "spt", b))
                    k = take(pe, (kind + "so", b))
                    nat = natc[b % 2] if kind == "m" else natv[b % 2]
                    own = ckv_nat if kind == "m" else v_nat
                    for c in range(2 if kind == "m" else 1):
                        for p in range(NPG):
                            mm(k[:, c * 32:(c + 1) * 32], nat[:, p, c * 128:(c + 1) * 128], pt_s[:, p, :], p == 0, False)
                        i = mm(k[:, c * 32:(c + 1) * 32], own[0:32, 2, c * 128:(c + 1) * 128], pt_s[0:32, NPG, :], False, True)
                    full(i, (kind + "so", b))

                wexp_ready.wait(pe, 0)
                k = take(pe, ("wcol",))
                for b in range(NB):
                    i = mm(k[0:32, b:b + 1], wexp[:, b, :], ones[:, :])
                full(i, ("wcol",))
                read_done(pe, ("ql", 2, 3))
                read_done(pe, ("qq", 2, 1))
                for b in range(NB):
                    transposed("m", b)
                    read_done(pe, ("pc", b, NPG - 2))
                    read_done(pe, ("pk", b, 1))
                    for u, (c0, w) in enumerate(UC):
                        k = take(pe, ("ms", b, u))
                        keys = ckp_t[:, :, c0:c0 + w] if u < 2 else ckv_t[:, :, new]
                        kr = kkp_t[IDX:QKD, c0:c0 + w] if u < 2 else kk_t[IDX:QKD, new]
                        mm(k[0:32, 0:w], ql_s[:, 0, b, :], keys[:, 0, :], True, False)
                        mm(k[0:32, 0:w], ql_s[:, 1, b, :], keys[:, 1, :], False, False)
                        full(mm(k[0:32, 0:w], qq_s[IDX:QKD, b, :], kr, False, True), ("ms", b, u))
                    for u, (c0, w) in enumerate(UC):
                        k = take(pe, ("is", b, u))
                        ki = kkp_t[0:IDX, c0:c0 + w] if u < 2 else kk_t[0:IDX, new]
                        full(mm(k[0:32, 0:w], qq_s[0:IDX, b, :], ki), ("is", b, u))
                    read_done(pe, ("is", b, 2))
                    for u, (c0, w) in enumerate(UC):
                        k = take(pe, ("ir", b, u))
                        full(mm(k[0:32, 0:w], rowsum[:, b, :], a_s[:, c0:c0 + w]), ("ir", b, u))
                    attend("m", b)
                read_done(pe, ("mso", NB - 1))
                values_up(2)
                sel_ready.wait(pe, 0)
                for b in range(NB):
                    transposed("d", b)
                    read_done(pe, ("pb", b, 1))
                    for u, (c0, w) in enumerate(UC):
                        k = take(pe, ("ds", b, u))
                        keys = ckp_t[:, 0, c0:c0 + w] if u < 2 else kb_t[:, new]
                        mm(k[0:32, 0:w], qblk[:, b, :], keys, True, False)
                        full(mm(k[0:32, 0:w], rep[:, b, :], wrk_s[:, c0:c0 + w], False, True), ("ds", b, u))
                    attend("d", b)

            for g, ts in enumerate(GROUPS):
                meet(pe, ("group", g))
                for t in ts:
                    xn_ready.wait(pe, t)
                    transpose_x(t, "x")
                for c in range(4):
                    w = chunk_wait((g, "in", c))
                    for t in ts:
                        if c == 0:
                            read_done(pe, ("x", t, 1))
                        b = take(pe, ("z", c, t))
                        for k in range(8):
                            i = mm(b[0:P[t], 0:ZC[c]], xt[IN_GROUP[t]][:, k, 0:P[t]], w[:, k, 0:ZC[c]], k == 0, k == 7)
                        full(i, ("z", c, t))
                for t in ts:
                    meet(pe, ("tile", t))
                    heads_part(t)
                    if t < 2:
                        prompt(t)
                    else:
                        meet(pe, ("sample",))
                        sample()
                meet(pe, ("out", g))
                for c in range(2):
                    w = chunk_wait((g, "out", c))
                    for t in ts:
                        b = take(pe, ("wo", c, t))
                        for k in range(8):
                            i = mm(b[0:P[t], :], mix_t[IN_GROUP[t]][:, k, 0:P[t]], w[:, k, :], k == 0, k == 7)
                        full(i, ("wo", c, t))
                for t in ts:
                    xn2_ready.wait(pe, t)
                    transpose_x(t, "x2")
                for c in range(4):
                    w = chunk_wait((g, "pq", c))
                    for t in ts:
                        n = P[t]
                        if c == 0:
                            read_done(pe, ("x2", t, 1))
                        b = take(pe, ("pq", c, t))
                        for j in range(4):
                            for k in range(8):
                                i = mm(b[:, j * n:(j + 1) * n], w[:, k, j * 128:(j + 1) * 128],
                                       xt[IN_GROUP[t]][:, k, 0:n], k == 0, k == 7)
                        full(i, ("pq", c, t))
                    for t in ts:
                        n = P[t]
                        read_done(pe, ("pq", c, t))
                        b = take(pe, ("sc", c, t))
                        for j in range(4):
                            i = mm(b[0:n, j * 128:(j + 1) * 128], qp_t[IN_GROUP[t]][:, j, 0:n], keys_t[:, 4 * c + j, :])
                        full(i, ("sc", c, t))
            meet(pe, 'experts')
            experts_pe(pe)

        @block.scalar
        def _(act):
            def copy(name, o, i, last=True):
                c = A.activation(o, i, ACT.Copy)
                if last:
                    drained(c, name)

            for c in range(4):
                b = ready(act, ("keys", c))
                copy(("keys", c), keys_t[:, 4 * c:4 * c + 4, :], b[:, :].rearrange("p (a b) -> p a b", b=128))
            for c in range(2):
                b = ready(act, ("uk", c))
                copy(("uk", c), uk_t[:, :, c * 128:(c + 1) * 128], b[:, :].rearrange("p (a b) -> p a b", b=128))
            for h in range(NH):
                b = ready(act, ("bias_d", h))
                copy(("bias_d", h), gd[:, h, :], b[:, 0:WD])
            for c in range(3):
                w = min(512, WS - 512 * c)
                b = ready(act, ("bias_s", c))
                copy(("bias_s", c), gs[:, c * 512:c * 512 + w], b[0:32, 0:w])
            act.wait_ge(scr_d_out, 16)
            act.wait_ge(scr_s_out, 16)

            def root(step, cols=slice(4, 5)):
                s = small[0:P[step[1]], cols]
                square_ready.wait(act, step)
                root_ready.send(A.activation(s, s, ACT.Sqrt), step)

            def split(a, m, n):
                return a.rearrange("p (a b) -> p a b", a=m)[:, :, 0:n]

            def x_evac(what, t):
                for c in range(2):
                    b = ready(act, (what, t, c))
                    copy((what, t, c), xt[IN_GROUP[t]][:, 4 * c:4 * c + 4, :], split(b[:, 0:4 * P[t]], 4, P[t]))

            def heads_part(t):
                n, r0 = P[t], ROW0[t]
                b = ready(act, ("cq", t))
                copy(("cq", t), cq_t[:, :, 0:n], split(b[:, 0:3 * n], 3, n))
                b = ready(act, ("kv", t))
                copy(None, ckv_t[:, :, r0:r0 + n], split(b[:, 0:256], 2, n), False)
                copy(None, kk_t[:, r0:r0 + n], b[0:QKD, 256:256 + n], False)
                copy(("kv", t), kb_t[:, r0:r0 + n], b[:, 384:384 + n])
                b = ready(act, ("qb", t))
                copy(("qb", t), qb_t[:, :, 0:n], split(b[:, 0:4 * n], 4, n))
                for c in range(2):
                    b = ready(act, ("q", t, c))
                    heads = b[0:n, 0:384].rearrange("p (h d) -> p h d", d=QKD)
                    copy(None, q_nope[0:n, c * 256:(c + 1) * 256].rearrange("p (h d) -> p h d", d=NOPE),
                         heads[:, :, 0:NOPE], False)
                    copy(("q", t, c), q_rope[0:n, c * 128:(c + 1) * 128].rearrange("p (h d) -> p h d", d=ROPE),
                         heads[:, :, NOPE:QKD])
                b = ready(act, ("qn", t))
                copy(("qn", t), qn_t[:, :, 0:n], split(b[:, 0:4 * n], 4, n))
                for c in range(2):
                    b = ready(act, ("qq", t, c))
                    if t < 2:
                        copy(("qq", t, c), qq_t[:, 4 * c:4 * c + 4, 0:n], split(b[0:QKD, 0:4 * n], 4, n))
                    else:
                        copy(("qq", t, c), free(qq_s[:, 0, 16 * c:16 * c + 1], (NT, 4), (32, NB), (1, NT)),
                             free(b[0:QKD, 0:1], (32, 4), (NT, NB), (1, NT)))
                for u in range(4):
                    b = ready(act, ("ql", t, u))
                    h = 4 * (u // 2) + u % 2
                    if t < 2:
                        copy(("ql", t, u), ql_t[:, :, h:h + 3:2, 0:n],
                             b[:, 0:4 * n].rearrange("p (c j n) -> p c j n", c=2, j=2))
                    else:
                        for c in range(2):
                            copy(("ql", t, u), free(ql_s[:, c, 0, NT * h:NT * h + 1], (2 * NT, 2), (32, NB), (1, NT)),
                                 free(b[:, 64 * c:64 * c + 1], (32, 2), (NT, NB), (1, NT)), c == 1)

            def prompt(t):
                nk = 128 * (t + 1)
                hp = 512 // nk
                steps = [(k, g) for k in "md" for g in range(HG[t])]
                for g in range(HG[t]):
                    b = ready(act, ("idx", t, g))
                    if g >= 2:
                        relu_used.wait(act, (t, g - 2))
                    drained(A.activation(relu[g % 2][:, :], b[:, :], ACT.Relu), ("idx", t, g))

                def exps(kind, g):
                    logits_sb.wait(act, (kind, t, g))
                    for j in range(hp):
                        s = s_b[g % 2][:, j * nk:(j + 1) * nk]
                        i = A.activation(s, s, ACT.Exp, bias=small[:, 32 + 8 * (g % 2) + j:33 + 8 * (g % 2) + j],
                                         accum_out=small[:, 48 + 8 * (g % 2) + j:49 + 8 * (g % 2) + j])
                    exps_ready.send(i, (kind, t, g))

                def after(kind, g):
                    b = ready(act, (kind + "pt", t, g))
                    n = steps.index((kind, g))
                    if n >= 2:
                        k2, g2 = steps[n - 2]
                        ready(act, ("ol", t, g2, 1) if k2 == "m" else ("od", t, g2))
                    copy((kind + "pt", t, g), p_t[g % 2][:, :], b[:, :])
                    if kind == "m":
                        for c in range(2):
                            b = ready(act, ("ol", t, g, c))
                            copy(("ol", t, g, c), o_t[:, c, g * hp:(g + 1) * hp, :],
                                 b[:, 0:hp * 128].rearrange("p (a b) -> p a b", b=128))
                    else:
                        b = ready(act, ("od", t, g))
                        g2, r = g * hp // HR, g * hp % HR
                        copy(("od", t, g), mix_t[IN_GROUP[t]][g2 * 64:g2 * 64 + 64, 4 + r:4 + r + hp, :],
                             b[g2 * 64:g2 * 64 + 64, 0:hp * 128].rearrange("p (a b) -> p a b", b=128))

                for kind in "md":
                    for g in range(HG[t] + 1):
                        if g < HG[t]:
                            exps(kind, g)
                        if g:
                            after(kind, g - 1)
                    if kind == "m":
                        b = ready(act, ("uv", t))
                        copy(("uv", t), mix_t[IN_GROUP[t]][:, 0:4, :], b[:, :].rearrange("p (a b) -> p a b", b=128))

            def sample():
                b_ = ready(act, ("wcol",))
                copy(("wcol",), wcol[:, :], b_[0:32, 0:NB])

                def softmax(kind, b):
                    logits_sb.wait(act, (kind, b))
                    exps_ready.send(A.activation(s_s[:, :], s_s[:, :], ACT.Exp, bias=small[0:32, 32:33],
                                                 accum_out=small[0:32, 48:49]), (kind, b))
                    k = ready(act, (kind + "spt", b))
                    if b:
                        ready(act, (kind + "so", b - 1))
                    elif kind == "d":
                        ready(act, ("mso", NB - 1))
                    copy(None, pt_s[:, 0:NPG, :], k[:, 0:256].rearrange("p (a b) -> p a b", b=32), False)
                    copy((kind + "spt", b), pt_s[0:32, NPG, :], k[0:32, 256:288])

                for b in range(NB):
                    qr = slice(NT * b, NT * b + NT)
                    for p in range(0, NPG, 2):
                        k = ready(act, ("pc", b, p))
                        if b and p == 0:
                            ready(act, ("ms", b - 1, 1))
                        copy(("pc", b, p), ckp_t[:, :, p * 128:(p + 2) * 128], split(k[:, :], 2, 256))
                    for c in range(2):
                        k = ready(act, ("pk", b, c))
                        if b and c == 0:
                            ready(act, ("is", b - 1, 1))
                        copy(("pk", b, c), kkp_t[0:QKD, c * 512:(c + 1) * 512], k[0:QKD, :])
                    softmax("m", b)
                    k = ready(act, ("mso", b))
                    for c in range(2):
                        i = A.activation(o_t[:, c, :, qr], k[:, c * 32:(c + 1) * 32].rearrange("p (h t) -> p h t", h=NH),
                                         ACT.Copy)
                        if c == 0:
                            lat_used.send(i, b)
                    drained(i, ("mso", b))
                k = ready(act, ("uv", 2))
                copy(("uv", 2), mix_t[1][:, 0:4, :], split(k[:, 0:128], 4, 32))
                for b in range(NB):
                    qr = slice(NT * b, NT * b + NT)
                    for c in range(2):
                        k = ready(act, ("pb", b, c))
                        if b and c == 0:
                            ready(act, ("ds", b - 1, 1))
                        copy(("pb", b, c), ckp_t[:, 0, c * 512:(c + 1) * 512], k[:, :])
                    softmax("d", b)
                    k = ready(act, ("dso", b))
                    for g2 in range(KG):
                        i = A.activation(mix_t[1][g2 * 64:g2 * 64 + 64, 4:8, qr],
                                         k[g2 * 64:g2 * 64 + 64, g2 * 16:g2 * 16 + 16]
                                         .rearrange("p (h t) -> p h t", h=HR), ACT.Copy)
                        if g2 == 0:
                            kv_used.send(i, b)
                    drained(i, ("dso", b))

            for g, ts in enumerate(GROUPS):
                meet(act, ("group", g))
                for t in ts:
                    root(("x", t))
                for t in ts:
                    x_evac("x", t)
                for c in range(4):
                    for t in ts:
                        b = ready(act, ("z", c, t))
                        copy(("z", c, t), z[IN_GROUP[t]][0:P[t], c * 512:c * 512 + ZC[c]], b[0:P[t], 0:ZC[c]])
                for t in ts:
                    meet(act, ("tile", t))
                    root(("z", t), slice(0, 2))
                    heads_part(t)
                    if t < 2:
                        prompt(t)
                        act.wait_ge(stored_z, 80 * (t + 1))
                    else:
                        act.wait_ge(stored_z, 80 * (t + 1))
                        meet(act, ("sample",))
                        sample()
                meet(act, ("out", g))
                for t in ts:
                    root(("h", t))
                for t in ts:
                    x_evac("x2", t)
                for c in range(4):
                    for t in ts:
                        n = P[t]
                        b = ready(act, ("pq", c, t))
                        if c:
                            ready(act, ("sc", c - 1, t))
                        copy(("pq", c, t), qp_t[IN_GROUP[t]][:, :, 0:n], split(b[:, 0:4 * n], 4, n))
                for t in ts:
                    gate_sub.wait(act, t)
                    gate_exp.send(A.activation(gt[0:P[t], :, :], gt[0:P[t], :, :], ACT.Exp), t)
            meet(act, "experts")
            for t in tiles:
                with act.Fori(0, GRAN[t] // D) as it:
                    for d in range(D):
                        n = BASE[t] + it * D + d
                        act.wait_ge(dots_done, n + (1 + D))
                        act.wait_ge(sums_done, n + 1)
                        A.sem_inc(gate_a, 1)
                        A.activation(wts[:, d, :], dots[:, d, :], ACT.Gelu).then_inc(gelu_done, 1)
                        act.wait_ge(gelu_done, n + 1)
                        A.sem_inc(gate_a, 1)
                        for j in range(G):
                            i = A.activation(dots[:, d, j:j + 1], wts[:, d, j:j + 1], ACT.Copy,
                                             scale=gate[t][:, bass.ds((it * D + d) * G + j, 1)])
                        i.then_inc(wts_done, 1)
                        act.wait_ge(wts_done, n + 1)
                        for j in range(G):
                            i = A.activation(d_ring[d * G + j][:, :], (ident if t < 2 else sel_sample)[:, :], ACT.Copy,
                                             scale=dots[:, d, j:j + 1])
                        i.then_inc(diag_done, 1)
                root(("y", t))

        @block.vector
        def _(dve):
            def mean_square(src, width, col, junk):
                n = src.shape[0]
                a = small[0:n, col:col + 1]
                link(V, V.tensor_tensor_reduce(out=junk, in0=src, in1=src, scale=1.0, scalar=0.0, op0=ALU.mult,
                                               op1=ALU.add, accum_out=a))
                return V.tensor_scalar(a, a, 1.0 / width, EPS, ALU.mult, ALU.add)

            def norm(src, gain, o, col):
                a = small[0:src.shape[0], col:col + 1]
                return V.scalar_tensor_tensor(out=o, in0=src, scalar=a, in1=gain, op0=ALU.mult, op1=ALU.mult)

            def rms(src, gain, o, step, sig, t):
                square_ready.send(mean_square(src, DM, 4, o), step)
                root_ready.wait(dve, step)
                a = small[0:src.shape[0], 4:5]
                link(V, V.reciprocal(a, a))
                sig.send(norm(src, gain, o, 4), t)
                sig.wait(dve, t)

            def rope(t, src, heads, stride, o, o_stride):
                n = P[t]
                cc = free(ropet[0:n, t, 0:1], (0, heads), (1, 32))
                for half in range(2):
                    other = src.offset + 16 * (1 - half)
                    V.tensor_tensor(rope_b[0:n, 0:heads, 16 * half:16 * half + 16],
                                    bass.AP(src.tensor, other, [list(src.ap[0]), [stride, heads], [1, 16]]),
                                    free(ropet[0:n, t, 32 + 16 * half:33 + 16 * half], (0, heads), (1, 16)), ALU.mult)
                link(V, V.tensor_tensor(rope_a[0:n, 0:heads, :], free(src, (stride, heads), (1, 32)), cc, ALU.mult))
                return V.tensor_tensor(free(o, (o_stride, heads), (1, 32)), rope_a[0:n, 0:heads, :],
                                       rope_b[0:n, 0:heads, :], ALU.add)

            dve.wait_ge(setup_in, SETUP_IN)
            V.tensor_copy(relb_x[:, :, :], free(relb[:, 0:1], (1, NH), (0, 128)))
            relb_ready.send(V.tensor_copy(relb_s[:, :, :], free(relb[:, 0:1], (1, NH), (0, NT))), 0)
            V.memset(x[2][:, :], 0.0).then_inc(x2_zero, 1)
            dve.wait_ge(consts_in, CONSTS_IN)
            dve.wait_ge(bias_in, 16 * (NH + 1))
            V.tensor_copy(free(bias_s[:, PAST + NT:PAST + NT + 1], (NT, NB - 1), (1, NT)),
                          free(bias_s[:, PAST:PAST + 1], (0, NB - 1), (1, NT)))

            def post(t):
                n, zt = P[t], z[IN_GROUP[t]]
                read_done(dve, ("z", 3, t))
                link(V, V.tensor_copy(v_nat[0:n, t, :], zt[0:n, O_VB:O_VB + 128]))
                z_q, z_kv = zt[0:n, O_CQ:O_CQ + QL], zt[0:n, O_CKV:O_CKV + KVL]
                mean_square(z_q, QL, 0, cqn[0:n, :])
                square_ready.send(mean_square(z_kv, KVL, 1, ckv_nat[0:n, t, :]), ("z", t))
                root_ready.wait(dve, ("z", t))
                link(V, V.reciprocal(small[0:n, 0:2], small[0:n, 0:2]))
                norm(z_q, g_q[0:n, :], cqn[0:n, :], 0)
                norm(z_kv, g_kv[0:n, :], ckv_nat[0:n, t, :], 1)
                link(V, rope(t, zt[0:n, O_KR:O_KR + 1], 1, 32, kk[0:n, IDX:IDX + 1], 32))
                link(V, rope(t, zt[0:n, O_KI:O_KI + 1], 1, 32, kk[0:n, 0:1], 32))
                V.tensor_copy(kk[0:n, 32:IDX], zt[0:n, O_KI + 32:O_KI + IDX])
                V.tensor_scalar(small[0:n, 16:24], zt[0:n, O_WI:O_WI + NH], IDX_W, None, ALU.mult)
                for r in range(HR):
                    V.tensor_copy(free(qb_pairs[0:n, r * 128:r * 128 + 1], (64, 2), (1, 64)),
                                  free(zt[0:n, O_QB + r * HD:O_QB + r * HD + 1], (HR * HD, 2), (1, HD)))
                link(V, rope(t, zt[0:n, O_QI:O_QI + 1], NH, IDX, qq[0:n, 0, 0:1], QKD))
                post_ready.send(V.tensor_copy(qq[0:n, :, 32:IDX],
                                              free(zt[0:n, O_QI + 32:O_QI + 33], (IDX, NH), (1, 32))), t)
                post_ready.wait(dve, t)
                read_done(dve, ("q", t, 1))
                qrope_ready.send(rope(t, q_rope[0:n, 0:1], NH, ROPE, qq[0:n, 0, IDX:IDX + 1], QKD), t)

            def normalise(key, s, width, heads, n, c):
                exps_ready.wait(dve, key)
                rec = small[0:n, 64 + c:64 + c + heads]
                link(V, V.reciprocal(rec, small[0:n, 48 + c:48 + c + heads]))
                if heads == 1:
                    i = V.tensor_scalar(s, s, rec, None, ALU.mult)
                else:
                    v = s.rearrange("p (a b) -> p a b", a=heads)
                    i = V.tensor_tensor(v, v, free(rec, (1, heads), (0, width)), ALU.mult)
                probs_ready.send(i, key)

            def prompt(t):
                nk = 128 * (t + 1)
                hp = 512 // nk
                mask = tri[:, 256 - nk:256]
                first = mask
                for g in range(HG[t]):
                    read_done(dve, ("idx", t, g))
                    for j in range(hp):
                        h = g * hp + j
                        i = V.scalar_tensor_tensor(out=iscore[:, 0:nk], in0=relu[g % 2][:, j * nk:(j + 1) * nk],
                                                   scalar=small[:, 16 + h:17 + h], in1=first, op0=ALU.mult, op1=ALU.add)
                        first = iscore[:, 0:nk]
                        if j < hp - 1:
                            link(V, i)
                        else:
                            relu_used.send(i, (t, g))
                            relu_used.wait(dve, (t, g))
                src = iscore[:, 0:nk]
                for r in range(TOPK_P // 8):
                    link(V, V.max(small[:, 24:32], src))
                    link(V, V.match_replace(out=iwork[:, 0:nk], in_to_replace=small[:, 24:32], in_values=src,
                                            imm_value=TAKEN))
                    src = iwork[:, 0:nk]
                link(V, V.tensor_scalar(iscore[:, 0:nk], src, TAKEN, -NEG, ALU.is_equal, ALU.mult))
                link(V, V.scalar_tensor_tensor(out=iscore[:, 0:nk], in0=iscore[:, 0:nk], scalar=NEG, in1=mask,
                                               op0=ALU.add, op1=ALU.add))
                link(V, V.tensor_tensor(bm[:, :, 0:nk], bias_d[:, :, 256 - nk:256],
                                        free(iscore[:, 0:1], (0, NH), (1, nk)), ALU.add))
                steps = [(k, g) for k in "md" for g in range(HG[t])]

                def logits(kind, g):
                    b = ready(dve, (kind, t, g))
                    n = steps.index((kind, g))
                    if n >= 2:
                        k2, g2 = steps[n - 2]
                        ready(dve, (k2 + "pt", t, g2))
                    s = s_b[g % 2]
                    add = free(mask, (0, hp), (1, nk)) if kind == "m" else bm[:, g * hp:(g + 1) * hp, 0:nk]
                    drained(V.scalar_tensor_tensor(
                        out=s.rearrange("p (a b) -> p a b", a=hp), in0=b[:, :].rearrange("p (a b) -> p a b", a=hp),
                        scalar=MLA_SCALE if kind == "m" else DSA_SCALE, in1=add, op0=ALU.mult, op1=ALU.add), (kind, t, g))
                    read_done(dve, (kind, t, g))
                    c = 8 * (g % 2)
                    logits_sb.send(V.tensor_reduce(out=small[:, 32 + c:32 + c + hp],
                                                   in_=s.rearrange("p (a b) -> p a b", a=hp), axis=AX.X, op=ALU.max,
                                                   negate=True), (kind, t, g))

                for kind in "md":
                    for g in range(HG[t] + 1):
                        if g < HG[t]:
                            logits(kind, g)
                        if g:
                            normalise((kind, t, g - 1), s_b[(g - 1) % 2], nk, hp, 128, 8 * ((g - 1) % 2))

            def sample():
                wexp_ready.send(V.tensor_tensor(free(wexp[:, 0, 0:1], (32, NB), (NT, NH), (1, NT)),
                                                free(small[0:32, 16:17], (0, NB), (1, NH), (0, NT)),
                                                free(rep[:, 0, 0:1], (32, NB), (NT, NH), (1, NT)), ALU.mult), 0)
                link(V, V.memset(qblk[:, :, :], 0.0))
                for g2 in range(KG):
                    q = slice(g2 * 64, g2 * 64 + 64)
                    V.tensor_copy(free(qblk[q, 0, g2 * 16:g2 * 16 + 1], (32, NB), (NT, HR), (1, NT)),
                                  free(qb_t[q, 0, 0:1], (NT, NB), (128, HR), (1, NT)))
                V.memset(i_s[:, 0:PAST], 0.0)
                link(V, V.tensor_copy(i_s[:, PAST:SK], newmask_i[:, :]))
                read_done(dve, ("wcol",))

                def logits(kind, b):
                    for u, (c0, w) in enumerate(UC):
                        k = ready(dve, (kind + "s", b, u))
                        if u == 0:
                            if b:
                                ready(dve, (kind + "spt", b - 1))
                            elif kind == "d":
                                ready(dve, ("mspt", NB - 1))
                        o, i = s_s[:, c0:c0 + w], k[0:32, 0:w]
                        if kind == "d":
                            y = V.scalar_tensor_tensor(out=o, in0=i, scalar=DSA_SCALE, in1=bias_s[:, c0:c0 + w],
                                                       op0=ALU.mult, op1=ALU.add)
                        elif u < 2:
                            y = V.tensor_scalar(o, i, MLA_SCALE, None, ALU.mult)
                        else:
                            y = V.scalar_tensor_tensor(out=o, in0=i, scalar=MLA_SCALE, in1=newmask[:, b, :],
                                                       op0=ALU.mult, op1=ALU.add)
                        drained(y, (kind + "s", b, u))
                    for u in range(3):
                        read_done(dve, (kind + "s", b, u))
                    logits_sb.send(V.tensor_reduce(out=small[0:32, 32:33], in_=s_s[:, :], axis=AX.X, op=ALU.max,
                                                   negate=True), (kind, b))

                for b in range(NB):
                    logits("m", b)
                    for u, (c0, w) in enumerate(UC):
                        k = ready(dve, ("is", b, u))
                        if b and u == 0:
                            ready(dve, ("ir", b - 1, 2))
                        drained(V.tensor_scalar(a_s[:, c0:c0 + w], k[0:32, 0:w], 0.0, wcol[:, b:b + 1], ALU.max, ALU.mult),
                                ("is", b, u))
                    for u, (c0, w) in enumerate(UC):
                        k = ready(dve, ("ir", b, u))
                        drained(V.tensor_tensor(i_s[:, c0:c0 + w], i_s[:, c0:c0 + w], k[0:32, 0:w], ALU.add), ("ir", b, u))
                    normalise(("m", b), s_s, SK, 1, 32, 0)
                    for u in range(3):
                        read_done(dve, ("ir", b, u))
                src = i_s
                for r in range(TOPK_S // 8):
                    link(V, V.max(small[0:32, 24:32], src))
                    link(V, V.match_replace(out=wrk_s, in_to_replace=small[0:32, 24:32], in_values=src, imm_value=TAKEN))
                    src = wrk_s
                link(V, V.tensor_scalar(wrk_s, wrk_s, TAKEN, -NEG, ALU.is_equal, ALU.mult))
                sel_ready.send(V.tensor_scalar(wrk_s, wrk_s, NEG, None, ALU.add), 0)
                for b in range(NB):
                    logits("d", b)
                    normalise(("d", b), s_s, SK, 1, 32, 0)

            def top16(score, work, values, index, last=None):
                m = len(score)
                for j in range(m):
                    i = V.max(values[j][:, 0:8], score[j])
                link(V, i)
                for j in range(m):
                    V.max_index(index[j][:, 0:8], values[j][:, 0:8], score[j])
                    i = V.match_replace(out=work[j], in_to_replace=values[j][:, 0:8], in_values=score[j], imm_value=TAKEN)
                if last:
                    drained(i, last)
                    read_done(dve, last)
                else:
                    link(V, i)
                for j in range(m):
                    i = V.max(values[j][:, 8:16], work[j])
                link(V, i)
                for j in range(m):
                    i = V.max_index(index[j][:, 8:16], values[j][:, 8:16], work[j])
                link(V, i)

            def choose(t):
                n, k = P[t], IN_GROUP[t]
                link(V, V.tensor_tensor(cand[0:n, :, :].rearrange("p h (a b) -> p h a b", a=16),
                                        free(sv[k][0:n, 0, 0:1], (32, NH), (1, 16), (0, 16)),
                                        free(sv[k][0:n, 1, 0:1], (32, NH), (0, 16), (1, 16)), ALU.add))
                hs = range(NH)
                c_ = [cand[0:n, h, :] for h in hs]
                top16(c_, c_, [cv[0:n, h, :] for h in hs], [ci[0:n, h, :] for h in hs])
                gate_sub.send(V.tensor_tensor(gt[0:n, :, :], cv[0:n, :, :], free(cv[0:n, 0, 0:1], (PTOP, NH), (0, PTOP)),
                                              ALU.subtract), t)
                V.tensor_copy(si[0:n, :, :], si_u[k][0:n, :, :])
                for half, (op, imm, e) in enumerate(((ALU.logical_shift_right, 4, ea), (ALU.bitwise_and, 15, eb))):
                    link(V, V.tensor_scalar(ca[0:n, :, :], ci[0:n, :, :], imm, None, op))
                    link(V, V.tensor_tensor(hot[0:n, :, :], free(ca[0:n, 0, 0:1], (1, NH * PTOP), (0, 16)),
                                            free(iota16[0:n, 0:1], (0, NH * PTOP), (1, 16)), ALU.is_equal))
                    hv = free(hot[0:n, 0, 0:1], (256, NH), (16, PTOP), (1, 16))
                    link(V, V.tensor_tensor(hv, hv, free(si[0:n, half, 0:1], (32, NH), (0, PTOP), (1, 16)), ALU.mult))
                    link(V, V.tensor_reduce(out=e[0:n, :], in_=hot[0:n, :, :], axis=AX.X, op=ALU.add))
                o = eid[t] if t < 2 else eu
                link(V, V.scalar_tensor_tensor(out=o[0:n, :], in0=ea[0:n, :], scalar=float(KEYS), in1=eb[0:n, :],
                                               op0=ALU.mult, op1=ALU.add))
                gate_exp.wait(dve, t)
                link(V, V.tensor_reduce(out=small[0:n, 96:104], in_=gt[0:n, :, :], axis=AX.X, op=ALU.add))
                link(V, V.reciprocal(small[0:n, 104:112], small[0:n, 96:104]))
                rc = free(small[0:n, 104:105], (1, NH), (0, PTOP))
                if t < 2:
                    slots_ready.send(V.tensor_tensor(gate[t][0:n, :].rearrange("p (h k) -> p h k", h=NH), gt[0:n, :, :],
                                                     rc, ALU.mult), t)
                else:
                    link(V, V.tensor_tensor(gt[0:n, :, :], gt[0:n, :, :], rc, ALU.mult))
                    gf = gt[0:n, :, :].rearrange("p h k -> p (h k)")
                    for q in range(4):
                        V.tensor_copy(gate[2][q * 32:q * 32 + 32, :], gf[:, q * 32:q * 32 + 32])
                        if q:
                            V.tensor_copy(xn2[2][q * 32:q * 32 + 32, :], xn2[2][0:32, :])
                        i = V.tensor_copy(eid[2][q * 32:q * 32 + 32, :], eu[0:32, q * 32:q * 32 + 32])
                    slots_ready.send(i, t)

            for g, ts in enumerate(GROUPS):
                meet(dve, ("group", g))
                for t in ts:
                    dve.wait_ge(x_in[t], 16)
                    zt = z[IN_GROUP[t]][0:P[t], 0:DM]
                    rms(x[t][0:P[t], :], g_attn[0:P[t], :], zt, ("x", t), xn_ready, t)
                for t in ts:
                    meet(dve, ("tile", t))
                    post(t)
                    if t < 2:
                        prompt(t)
                    else:
                        meet(dve, ("sample",))
                        sample()
                meet(dve, ("out", g))
                for c in range(2):
                    for t in ts:
                        b = ready(dve, ("wo", c, t))
                        h = x[t][0:P[t], c * 512:(c + 1) * 512]
                        drained(V.tensor_tensor(h, h, b[0:P[t], :], ALU.add), ("wo", c, t))
                for t in ts:
                    for c in range(2):
                        read_done(dve, ("wo", c, t))
                    rms(x[t][0:P[t], :], g_ffn[0:P[t], :], xn2[t][0:P[t], :], ("h", t), xn2_ready, t)
                for c in range(4):
                    for t in ts:
                        n, k = P[t], IN_GROUP[t]
                        b = ready(dve, ("sc", c, t))
                        top16([b[0:n, j * 128:(j + 1) * 128] for j in range(4)], [sc[0:n, j, :] for j in range(4)],
                              [sv[k][0:n, 4 * c + j, :] for j in range(4)], [si_u[k][0:n, 4 * c + j, :] for j in range(4)],
                              ("sc", c, t))
                for t in ts:
                    choose(t)
            meet(dve, "experts")
            for t in tiles:
                if t == 0:
                    V.memset(small[0:1, 120:121], 0.0).then_inc(dots_done, D)
                with dve.Fori(0, GRAN[t] // D) as it:
                    for d in range(D):
                        n = BASE[t] + it * D + d
                        dve.wait_ge(sums_done, n + 1)
                        for j in range(G):
                            k = d * G + j
                            dve.wait_ge(u_in[k], (it + (BASE[t] // D + 1)) * 16)
                            i = V.tensor_tensor_reduce(out=u_ring[k][:, :], in0=u_ring[k][:, :], in1=xn2[t][:, :],
                                                       scale=1.0, scalar=0.0, op0=ALU.mult, op1=ALU.add,
                                                       accum_out=dots[:, d, j:j + 1])
                        i.then_inc(dots_done, 1)
                dve.wait_ge(sums_done, BASE[t] + GRAN[t] + D)
                acc_read.send(V.tensor_copy(x[t][:, :], acc[:, :]), t)
                acc_read.wait(dve, t)
                n = P[t]
                if t == 0:
                    dve.wait_ge(gfin_in, 16)
                rms(x[t][0:n, :], g_fin[0:n, :], xn2[t][0:n, :], ("y", t), y_ready, t)

        @block.gpsimd
        def _(pool):
            pool.wait_ge(met, 3 * MEETINGS)
            for t in tiles:
                with pool.Fori(0, GRAN[t] // D) as it:
                    for d in range(D):
                        n = BASE[t] + it * D + d
                        pool.wait_ge(dots_done, n + 1)
                        pool.wait_ge(sums_done, n + 1)
                        nc.gpsimd.tensor_copy(stage[:, d, :], eid[t][:, bass.ds((it * D + d) * G, G)]).then_inc(staged, 1)
                        pool.wait_ge(staged, n + 1)
                        nc.gpsimd.sem_inc(gate_p, 1)
                        for ring, table, sems in ((u_ring, inp["peer_u"], u_in), (v_ring, inp["peer_v"], v_in)):
                            for j in range(G):
                                k = d * G + j
                                nc.gpsimd.indirect_dma_start(
                                    out=ring[k][:, :], out_offset=None, in_=table,
                                    in_offset=bass.IndirectOffsetOnAxis(ap=stage[:, d, j:j + 1], axis=0)
                                ).then_inc(sems[k], 16)

        @block.sync
        def _(sp):
            def load(o, i, s):
                sp.dma_start(o, i).then_inc(s, 16)

            def bcast(src, n):
                return bass.AP(src.tensor, src.offset, [[0, 128], [1, n]])

            sp.dma_start(x[0][:, :], inp["x_prompt"][0, 0:128, :]).then_inc(x_in[0], 16)
            early = [(ident[:, :], cst["ident"]), (g_attn[:, :], bcast(inp["g_attn"], DM)),
                     (tri[:, :], cst["tri"]), (sel_sample[:, :], cst["sel"]), (iota16[:, :], cst["iota"]),
                     (ropet[:, 0:2, :], cst["rope"][0:256, :].rearrange("(a p) c -> p a c", p=128)),
                     (ropet[0:32, 2, :], cst["rope"][256:288, :]),
                     (g_ffn[:, :], bcast(inp["g_ffn"], DM)), (g_q[:, :], bcast(inp["g_q"], QL)),
                     (g_kv[:, :], bcast(inp["g_kv"], KVL)), (newmask[:, :, :], cst["newmask"]),
                     (newmask_i[:, :], cst["newmask_i"]), (rep[:, :, :], cst["rep"]), (rowsum[:, :, :], cst["rowsum"]),
                     (ones[:, :], cst["ones"]),
                     (w_uq[:, :, :], inp["w_uq"][0].rearrange("(k p) n -> p k n", p=128)),
                     (w_uv[:, :, :], inp["w_uv"][0].rearrange("(k p) h v -> p k (h v)", p=128))]
            assert 16 * len(early) == CONSTS_IN
            setup = [(relb[:, :], inp["rel_bias"]), (hot_u[:, :], cst["hot"]),
                     (keys_nat[:, :, :], inp["peer_keys"][0].rearrange("h p k d -> k (h p) d")),
                     (uk_nat[:, :, :], inp["w_uk"][0].rearrange("(k p) h n -> p k (h n)", p=128))]
            assert 16 * len(setup) == SETUP_IN
            for o, i in early:
                load(o, i, consts_in)
            for o, i in setup:
                load(o, i, setup_in)
            load(page_sb[:, :], inp["page_table"].rearrange("(o b) p -> o (b p)", o=1), page_ids_in)

            def chunk(n):
                g, w, c = CHUNKS[n]
                slot, s = wring[n % NW], w_in_slot[n % NW]
                if w == "in":
                    load(slot[:, :, 0:ZC[c]], inp["w_in"][0, :, c * 512:c * 512 + ZC[c]]
                         .rearrange("(k p) n -> p k n", p=128), s)
                elif w == "out":
                    cols = slice(c * 512, (c + 1) * 512)
                    half = NH * VD
                    load(slot[:, 0:4, :], inp["w_out"][0, 0:half, cols].rearrange("(k p) n -> p k n", p=128), s)
                    for g2 in range(KG):
                        load(slot[g2 * 64:g2 * 64 + 64, 4:8, :],
                             inp["w_out"][0, half + g2 * 256:half + (g2 + 1) * 256, cols]
                             .rearrange("(r d) n -> d r n", d=64), s)
                else:
                    load(slot[:, :, :], inp["w_pq"][0, :, c * 512:(c + 1) * 512].rearrange("(k p) n -> p k n", p=128), s)

            def chunk_used(n):
                g, w, c = CHUNKS[n]
                ready(sp, ({"in": "z", "out": "wo", "pq": "pq"}[w], c, GROUPS[g][-1]))

            chunk(0)
            chunk(1)
            for t in (1, 2):
                if t == 2:
                    sp.wait_ge(x2_zero, 1)
                load(x[t][0:P[t], :], inp["x_prompt"][0, 128:256, :] if t == 1 else
                     inp["x_sample"].rearrange("b t d -> (b t) d"), x_in[t])
            read_done(sp, ("bias_d", NH - 1))
            sp.dma_start(scr_d, gd[:, :, :]).then_inc(scr_d_out, 16)
            read_done(sp, ("bias_s", 2))
            sp.dma_start(scr_s, gs[:, :]).then_inc(scr_s_out, 16)
            sp.wait_ge(scr_d_out, 16)
            sp.wait_ge(scr_s_out, 16)
            load(bias_d[:, :, :], bass.AP(scr_d.tensor, 127, [[NH * WD - 1, 128], [WD, NH], [1, 256]]), bias_in)
            for h in range(NH):
                load(bias_s[h * NT:(h + 1) * NT, 0:PAST + NT],
                     bass.AP(scr_s.tensor, h * NT * WS + NT - 1, [[WS - 1, NT], [1, PAST + NT]]), bias_in)

            def store_rows(t):
                n, zt = P[t], z[IN_GROUP[t]]
                post_ready.wait(sp, t)
                for name, src in (("ckv", ckv_nat[0:n, t, :]), ("kr", kk[0:n, IDX:QKD]), ("k", zt[0:n, O_KB:O_KB + 128]),
                                  ("v", zt[0:n, O_VB:O_VB + 128]), ("ki", kk[0:n, 0:IDX])):
                    o = out[name + "_p"][t * 128:(t + 1) * 128, :] if t < 2 else out[name + "_s"]
                    sp.dma_start(o, src).then_inc(stored_z, 16)

            def pages(which, i, par):
                for p in range(NPG):
                    ids = page_sb[0:1, bass.ds(i * (2 * NPG) + par * NPG + p, 1)] if not isinstance(i, int) else \
                        page_sb[0:1, (2 * i + par) * NPG + p:(2 * i + par) * NPG + p + 1]
                    pg = sp.value_load(ids, min_val=0, max_val=inp["cache_k"].shape[1] - 1)
                    if which == "lat":
                        moves = ((natc[par][:, p, :], inp["cache_ckv"]), (natk96[par][:, p, 0:IDX], inp["cache_kidx"]),
                                 (natk96[par][:, p, IDX:QKD], inp["cache_krope"]))
                    else:
                        moves = ((natk[par][:, p, :], inp["cache_k"]), (natv[par][:, p, :], inp["cache_v"]))
                    for o, table in moves:
                        tb = table[0]
                        if len(tb.shape) == 4:
                            tb = tb.rearrange("n p g d -> n p (g d)")
                        sp.dma_start(o, tb[bass.ds(pg, 1), :, :].rearrange("a p c -> p (a c)")).then_inc(
                            (lat_in if which == "lat" else kv_in)[par], 16)

            for n in range(2, 10):
                chunk_used(n - NW)
                chunk(n)
                if n == 3:
                    store_rows(0)
            for n in range(10, 14):
                chunk_used(n - NW)
                chunk(n)
            store_rows(1)
            sp.wait_ge(page_ids_in, 16)
            for par in range(2):
                chunk_used(12 + par)
                pages("lat", 0, par)
            store_rows(2)
            with sp.Fori(1, NB // 2) as i:
                for par in range(2):
                    sp.wait_ge(lat_used.sem, i * 2 + (par - 1))
                    pages("lat", i, par)
            for par in range(2):
                lat_used.wait(sp, NB - 2 + par)
                pages("kv", 0, par)
            with sp.Fori(1, NB // 2) as i:
                for par in range(2):
                    sp.wait_ge(kv_used.sem, i * 2 + (par - 1))
                    pages("kv", i, par)
            for n in range(14, 20):
                if n < 16:
                    kv_used.wait(sp, NB - 2 + n - 14)
                else:
                    chunk_used(n - NW)
                chunk(n)
            load(g_fin[:, :], bcast(inp["g_final"], DM), gfin_in)
            for t in tiles:
                y_ready.wait(sp, t)
                o = out["y_p"][t * 128:(t + 1) * 128, :] if t < 2 else out["y_s"]
                sp.dma_start(o, xn2[t][0:P[t], :]).then_inc(stored, 16)
            sp.wait_ge(stored, 48)
            sp.wait_ge(stored_z, 240)


def shape_constants():
    f = np.float32
    pos = np.concatenate([np.arange(SEQ), np.tile(PAST + np.arange(NT), NB)]).astype(f)
    inv = (f(10000.0) ** (-np.arange(16, dtype=f) / f(16))).astype(f)
    ang = pos[:, None] * inv
    cos, sin = np.cos(ang).astype(f), np.sin(ang).astype(f)
    dist = np.maximum(PAST + NT - 1 - np.arange(GU), 0)
    nf = np.maximum(dist, 1).astype(f)
    large = 16 + (np.log(nf / f(16)) / f(math.log(8.0)) * f(16)).astype(np.int32)
    bucket = np.where(dist < 16, dist, np.minimum(large, REL_B - 1))
    col = np.arange(256)[None, :] - 128
    r = np.arange(32)
    b, t = r // NT, r % NT
    ht = np.arange(32) % NT
    s = np.arange(NB)
    rep = (b[:, None, None] == s[None, :, None]) & (t[:, None, None] == ht[None, None, :])
    newmask = np.where((b[None, None, :] == s[None, :, None]) & (t[None, None, :] <= ht[:, None, None]), 0, NEG)
    newmask_i = np.where((b[None, :] == b[:, None]) & (t[None, :] <= t[:, None]), 0, NEG)
    sel = (np.arange(128)[:, None] % 32) == np.arange(128)[None, :]
    c = {
        "ident": np.eye(128),
        "tri": np.where(col <= np.arange(128)[:, None], 0, NEG),
        "sel": sel, "iota": np.tile(np.arange(16), (128, 1)),
        "rope": np.concatenate([cos, cos, -sin, sin], 1),
        "newmask": newmask, "newmask_i": newmask_i, "rep": rep, "rowsum": rep.transpose(2, 1, 0),
        "ones": np.ones((32, 1)), "hot": np.arange(REL_B)[:, None] == bucket[None, :],
    }
    return {k: np.ascontiguousarray(v, dtype=f) for k, v in c.items()}


INPUTS = ["x_prompt", "x_sample", "cache_ckv", "cache_krope", "cache_k", "cache_v", "cache_kidx", "page_table",
          "rel_bias", "g_attn", "w_in", "g_q", "w_uq", "g_kv", "w_uk", "w_uv", "w_out", "g_ffn", "w_pq", "peer_keys",
          "peer_u", "peer_v", "g_final"]
OUTPUTS = {"y_p": (SEQ, DM), "y_s": (32, DM), "ckv_p": (SEQ, KVL), "kr_p": (SEQ, ROPE), "k_p": (SEQ, 128),
           "v_p": (SEQ, 128), "ki_p": (SEQ, IDX), "ckv_s": (32, KVL), "kr_s": (32, ROPE), "k_s": (32, 128),
           "v_s": (32, 128), "ki_s": (32, IDX)}
SHAPES = [(1, SEQ, DM), (NB, NT, DM), (1, 1, SEQ, KVL), (1, 1, SEQ, ROPE), (1, 1, SEQ, KG, HD), (1, 1, SEQ, KG, HD),
          (1, 1, SEQ, IDX), (1, NB, NT, KVL), (1, NB, NT, ROPE), (1, NB, NT, KG, HD), (1, NB, NT, KG, HD),
          (1, NB, NT, IDX)]


def kernel(**inputs):
    import concourse.bacc as bacc
    from concourse.bass_utils import run_bass_kernel_spmd as run

    nc = bacc.Bacc("TRN2", target_bir_lowering=False, num_devices=1)
    arrays, inp, cst, out = {}, {}, {}, {}
    for name in INPUTS:
        a = np.ascontiguousarray(inputs[name])
        arrays[f"in_{name}"] = a
        inp[name] = nc.dram_tensor(f"in_{name}", a.shape, mybir.dt.from_np(a.dtype), kind="ExternalInput").ap()
    inp["peer_u"], inp["peer_v"] = (inp[n].rearrange("l e d -> (l e) d") for n in ("peer_u", "peer_v"))
    for name, a in shape_constants().items():
        arrays[f"const_{name}"] = a
        cst[name] = nc.dram_tensor(f"const_{name}", a.shape, F32, kind="ExternalInput").ap()
    for name, shape in OUTPUTS.items():
        out[name] = nc.dram_tensor(f"out_{name}", shape, F32, kind="ExternalOutput").ap()
    scr_d = nc.dram_tensor("bias_rows_prompt", (128, NH, WD), F32, kind="Internal").ap()
    scr_s = nc.dram_tensor("bias_rows_sample", (32, WS), F32, kind="Internal").ap()
    build(nc, inp, cst, out, scr_d, scr_s)
    r = run(nc, [arrays], core_ids=[0])
    return tuple(r.results[0][f"out_{n}"].reshape(s) for n, s in zip(OUTPUTS, SHAPES))
```

```python
import math
from contextlib import ExitStack

import numpy as np
import concourse.bass as bass
from concourse import mybir

F32 = mybir.dt.float32
U32 = mybir.dt.uint32
I32 = mybir.dt.int32
ALU = mybir.AluOpType
ACT = mybir.ActivationFunctionType
AX = mybir.AxisListType

DM, SEQ, NB, NT, PAST, PAGE = 1024, 256, 8, 4, 1024, 128
NPG = PAST // PAGE
NH, NOPE, ROPE, VD = 8, 64, 32, 64
QL, KVL = 384, 256
KG, HD = 2, 64
HR = NH // KG
IDX = 64
QKD = IDX + ROPE
EPS = 1e-6
MLA_SCALE = (NOPE + ROPE) ** -0.5
DSA_SCALE = HD ** -0.5
IDX_W = (NH * IDX) ** -0.5
TOPK_P, TOPK_S = 64, 256
REL_B = 32
KEYS, EXPERTS, PTOP = 128, 128 * 128, 16
P = [128, 128, NB * NT]
ROW0 = [0, 128, 256]
SPL = [QL, KVL, ROPE, NH * HD, KG * HD, KG * HD, NH * IDX, IDX, NH]
OFF = [sum(SPL[:i]) for i in range(len(SPL))]
O_CQ, O_CKV, O_KR, O_QB, O_KB, O_VB, O_QI, O_KI, O_WI = OFF
DIN = sum(SPL)
ZC = [512, 512, 512, DIN - 1536]
SK = PAST + NB * NT
UC = [(0, 512), (512, 512), (1024, NB * NT)]
NEG = -1e30
TAKEN = -3e38
GU = 1156
WD = 383
WS = 1031

FIRST_IN, CONSTS_IN, SETUP_IN = 16 * 2, 16 * 16, 16 * 4
NRING = 6
SHARED = 5760
NW = 2
CW = 256
RU, RV, RD = 5, 7, 3
RC = 8
W_IN, W_PQ, W_HEADS, W_PROMPT, W_MID = 1, 2, 4, 5, {"m": 4, "d": 2}
CHOOSE = [3] * 9
PRELOADED = 4
SLOTS = [128, 128, 32]
BASE = [sum(SLOTS[:t]) for t in range(3)]
FRONT = 5 * W_IN + 4 * W_HEADS + 8 * W_PQ + sum(CHOOSE)
SHARES = [0, FRONT + 12 + 10 * W_PROMPT, FRONT + 2 * (NB + 1) + 2 * NB * sum(W_MID.values()) + 9 * W_IN]


def free(ap, *dims):
    return bass.AP(ap.tensor, ap.offset, [list(ap.ap[0])] + [list(d) for d in dims])


def build(nc, inp, cst, out, scr_d, scr_s):
    ctx = ExitStack()
    with ctx:
        def sb(name, shape, dt=F32):
            return ctx.enter_context(nc.sbuf_tensor(name, shape, dt))

        def sem(name):
            return ctx.enter_context(nc.semaphore(name))

        ident = sb("ident", [128, 128])
        tri = sb("tri", [128, 256])
        sel_sample = sb("sel_sample", [128, 128])
        iota16 = sb("iota16", [128, 16])
        ropet = sb("ropet", [128, 3, 64])
        g_attn = sb("g_attn_sb", [128, DM])
        g_ffn = sb("g_ffn_sb", [128, DM])
        g_fin = sb("g_fin_sb", [128, DM])
        g_q = sb("g_q_sb", [128, QL])
        g_kv = sb("g_kv_sb", [128, KVL])
        newmask = sb("newmask", [32, NB, 32])
        newmask_i = sb("newmask_i", [32, 32])
        rep = sb("rep", [32, NB, 32])
        rowsum = sb("rowsum", [32, NB, 32])
        ones = sb("ones", [32, 1])
        page_sb = sb("page_sb", [1, NB * NPG], I32)
        w_uq = sb("w_uq_sb", [128, 3, NH * QKD])
        uk_t = sb("uk_t", [128, HR, KVL])
        w_uv = sb("w_uv_sb", [128, 2, NH * VD])
        keys_t = sb("keys_t", [128, 16, KEYS])
        bias_d = sb("bias_d", [128, NH, 256])
        bias_s = sb("bias_s", [32, SK])
        x_b = [sb(f"x{i}", [128, DM]) for i in range(2)]
        xn2_b = [sb(f"xn2_{i}", [128, DM]) for i in range(2)]
        x, xn2 = [x_b[t % 2] for t in range(3)], [xn2_b[t % 2] for t in range(3)]
        eid = [sb(f"eid{t}", [128, SLOTS[t]], U32) for t in range(3)]
        gate = [sb(f"gate{t}", [128, SLOTS[t]]) for t in range(3)]
        ckv_nat = sb("ckv_nat", [128, 3, KVL])
        v_nat = sb("v_nat", [128, 3, 128])
        ckv_t = sb("ckv_t", [128, 2, 288])
        kk_t = sb("kk_t", [QKD, 288])
        kb_t = sb("kb_t", [128, 288])
        small = sb("small", [128, 256])
        rows = sb("rows", [128, RU + RV, DM])
        u_ring = [rows[:, i, :] for i in range(RU)]
        v_ring_f = rows[:, RU:RU + 2, :].rearrange("p a b -> p (a b)")
        v_ring = [rows[:, RU + i, :] for i in range(RV)]
        d_ring = [sb(f"diag{i}", [128, 128]) for i in range(RD)]
        dots = sb("dots", [128, RC])
        gelus = sb("gelus", [128, RC])
        wts = sb("wts", [128, RC])
        wflat = sb("wring", [128, NW * 8 * CW])
        wring = [wflat[:, i * 8 * CW:(i + 1) * 8 * CW].rearrange("p (k c) -> p k c", c=CW) for i in range(NW)]
        zflat = sb("z", [128, 2048])
        z = zflat[:, 0:DIN]
        xt_f = sb("xt", [128, 1024])
        xt = [xt_f[:, 0:8 * P[t]].rearrange("p (k n) -> p k n", k=8) for t in range(3)]
        mix_f = sb("mix_t", [128, 1024])
        mix_t = [mix_f[:, 0:8 * P[t]].rearrange("p (k n) -> p k n", k=8) for t in range(3)]
        ql_f = sb("ql_t", [128, 2048])
        ql_t = ql_f[:, :].rearrange("p (c h n) -> p c h n", c=2, h=NH)
        qq_t = sb("qq_t", [QKD, NH, 128])
        qn_t = sb("qn_t", [128, HR, 128])
        qb_t = sb("qb_t", [128, HR, 128])
        cq_t = sb("cq_t", [128, 3, 128])
        qp_t = [qb_t, qn_t]
        shared = sb("shared", [128, SHARED])
        used = [0]

        def carve(base, at, parts, *shape):
            n = int(np.prod(shape))
            a = base[0:parts, at:at + n]
            if len(shape) == 1:
                return a
            names = "abc"[:len(shape)]
            return a.rearrange(f"p ({' '.join(names)}) -> p {' '.join(names)}", **dict(zip(names[1:], shape[1:])))

        def region(name, parts, *shape):
            used[0] += int(np.prod(shape))
            assert used[0] <= SHARED, (name, used)
            return carve(shared, used[0] - int(np.prod(shape)), parts, *shape)

        s_b = [region(f"s{i}", 128, 512) for i in range(2)]
        relu = [region(f"relu{i}", 128, 512) for i in range(2)]
        iscore = region("iscore", 128, 256)
        iwork = region("iwork", 128, 256)
        q_nope = region("q_nope", 128, NH * NOPE)
        q_rope = region("q_rope", 128, NH * ROPE)
        qb_pairs = relu[0]
        cqn = region("cqn", 128, QL)
        kk = region("kk", 128, QKD)
        rope_a = region("rope_a", 128, NH, 32)
        rope_b = region("rope_b", 128, NH, 32)
        qq = region("qq", 128, NH, QKD)
        p_t = [xt_f[:, i * 512:(i + 1) * 512] for i in range(2)]
        o_t = zflat[:, :].rearrange("p (c h n) -> p c h n", c=2, h=NH)
        pages_f = [zflat[:, :], wflat[:, 0:2048], wflat[:, 2048:4096]]
        nat_c = [f.rearrange("p (b c) -> p b c", c=256) for f in pages_f]
        nat_k = [f[:, 0:1024].rearrange("p (b c) -> p b c", c=128) for f in pages_f]
        nat_v = [f[:, 1024:2048].rearrange("p (b c) -> p b c", c=128) for f in pages_f]
        nat_r = [carve(mix_f, 256 * (i + 1), 128, NPG, ROPE) for i in range(3)]
        nat_i = [carve(wflat, 512 * i, 128, NPG, IDX) for i in range(NB)]
        used[0] = 0
        ckp_t = region("ckp_t", 128, 2, PAST)
        kr_t = region("kr_t", 128, PAST)
        ki_t = [ckp_t[0:IDX, i, :] for i in range(2)]
        s_s = [region(f"s_s{i}", 32, SK) for i in range(2)]
        pt_s = region("pt_s", 128, 9, 32)
        wexp = region("wexp", 32, NB, 32)
        wcol = region("wcol", 32, NB)
        ql_s = carve(ql_f, 0, 128, 2, NB, 32)
        i_s = carve(ql_f, 512, 32, SK)
        qq_s = qq_t[:, 0:2, :].rearrange("p h n -> p (h n)").rearrange("p (b q) -> p b q", q=32)
        o_s = carve(xt_f, 0, 128, 2, NH, 32)
        qblk = carve(xt_f, 512, 128, NB, 32)
        used[0] = 0
        sc = region("sc", 128, 4, KEYS)
        sv = region("sv", 128, 16, PTOP)
        si = region("si", 128, 16, PTOP)
        si_u = region("si_u", 128, 16, PTOP).bitcast(U32)
        cv = region("cv", 128, NH, PTOP)
        ci = region("ci", 128, NH, PTOP).bitcast(U32)
        ca = region("ca", 128, NH, PTOP).bitcast(U32)
        ea = region("ea", 128, NH * PTOP)
        eb = region("eb", 128, NH * PTOP)
        eu = region("eu", 128, NH * PTOP).bitcast(U32)
        gt = region("gt", 128, NH, PTOP)
        cands = [f.rearrange("p (h c) -> p h c", h=NH) for f in (v_ring_f[:, 0:2048], zflat[:, :], zflat[:, :])]
        hot = ql_f[:, :].rearrange("p (s c) -> p s c", c=16)
        rows_f = rows[:, :, :].rearrange("p a b -> p (a b)")
        setup_at = [0]

        def setup_buf(name, parts, *shape):
            setup_at[0] += int(np.prod(shape))
            return carve(rows_f, setup_at[0] - int(np.prod(shape)), parts, *shape)

        relb = setup_buf("relb", 32, NH)
        relb_x = setup_buf("relb_x", 32, NH, 128)
        relb_s = setup_buf("relb_s", 32, NH, NT)
        hot_u = setup_buf("hot_u", 32, GU)
        gd = setup_buf("gd", 128, NH, WD)
        gs = setup_buf("gs", 32, WS)
        keys_nat = setup_buf("keys_nat", 128, 16, 128)
        uk_nat = setup_buf("uk_nat", 128, 2, 512)

        acc = ctx.enter_context(nc.psum_tensor("acc", [128, DM], F32))
        banks = [ctx.enter_context(nc.psum_tensor(f"bank{i}", [128, 512], F32)) for i in range(NRING)]
        bank_full = [sem(f"bank{i}_full") for i in range(NRING)]
        bank_free = [sem(f"bank{i}_free") for i in range(NRING)]
        turn = {}

        def take(pe, name):
            n = turn[name] = len(turn)
            if n >= NRING:
                pe.wait_ge(bank_free[n % NRING], n // NRING)
            return banks[n % NRING]

        def full(ins, name):
            ins.then_inc(bank_full[turn[name] % NRING], 1)

        def ready(eng, name):
            n = turn[name]
            eng.wait_ge(bank_full[n % NRING], n // NRING + 1)
            return banks[n % NRING]

        def drained(ins, name):
            ins.then_inc(bank_free[turn[name] % NRING], 1)

        def read_done(eng, name):
            n = turn[name]
            eng.wait_ge(bank_free[n % NRING], n // NRING + 1)

        class Signal:

            def __init__(self, name, steps, unit=1):
                self.sem, self.unit, self.sent = sem(name), unit, 0
                self.at = {k: i + 1 for i, k in enumerate(steps)}

            def send(self, ins, step):
                self.sent += 1
                assert self.at[step] == self.sent, (self.at, step)
                ins.then_inc(self.sem, self.unit)

            def wait(self, eng, step):
                eng.wait_ge(self.sem, self.at[step] * self.unit)

        tiles = [0, 1, 2]
        first_in = sem("first_consts_in")
        consts_in = sem("consts_in")
        setup_in = sem("setup_in")
        small_w_in = sem("small_w_in")
        x_in = [sem(f"x{t}_in") for t in tiles]
        y_out = sem("y_stored")
        w_in_slot = [sem(f"w_slot{i}_in") for i in range(NW)]
        CHUNKS = [(t, w, c) for t in tiles for w, n in (("in", 8), ("out", 4), ("pq", 8)) for c in range(n)]
        W_DMAS = {"in": 1, "out": 3, "pq": 1}
        page_ids_in = sem("page_ids_in")
        idx_in = [sem(f"index_pages{b}_in") for b in range(NB)]
        lat_in = [sem(f"latent_pages{i}_in") for i in range(3)]
        kv_in = [sem(f"kv_pages{i}_in") for i in range(3)]
        lat_used = Signal("latent_pages_used", range(NB))
        kv_used = Signal("kv_pages_used", range(NB))
        scr_d_out, scr_s_out, bias_in = sem("scratch_d_out"), sem("scratch_s_out"), sem("bias_in")
        stored_z = sem("stored_z")
        met = sem("met")
        xn_ready = Signal("xn_ready", tiles)
        relb_ready = Signal("relb_ready", [0])
        post_ready = Signal("post_ready", tiles)
        qrope_ready = Signal("qrope_ready", tiles)
        HG = [NH * P[1] * (t + 1) // 512 for t in (0, 1)]
        probs_ready = Signal("probs_ready", [(k, t, g) for t in (0, 1) for k in "md" for g in range(HG[t])]
                             + [("m", b) for b in range(NB)] + [("d", b) for b in range(NB)])
        logits_sb = Signal("logits_sb", list(probs_ready.at))
        exps_ready = Signal("exps_ready", list(probs_ready.at))
        relu_used = Signal("relu_used", [(t, g) for t in (0, 1) for g in range(HG[t])])
        wexp_ready = Signal("wexp_ready", [0])
        sel_ready = Signal("sel_ready", tiles)
        w_even_used = Signal("w_even_used", [c for c in CHUNKS if c[2] % 2 == 0])
        xn2_ready = Signal("xn2_ready", tiles)
        ROOTS = [(w, t) for t in tiles for w, t in (("x", t), ("z", t), ("h", t)) + ((("y", t - 1),) if t else ())]
        ROOTS.append(("y", 2))
        square_ready = Signal("mean_square_ready", ROOTS)
        root_ready = Signal("root_ready", ROOTS)
        gate_sub = Signal("gate_sub", tiles)
        gate_exp = Signal("gate_exp", tiles)
        slots_ready = Signal("slots_ready", tiles)
        chain_v, chain_a = sem("vector_chain"), sem("scalar_chain")
        links = {"v": 0, "a": 0}
        meetings = {}

        def link(eng, ins):
            k, s = {id(nc.vector): ("v", chain_v), id(nc.scalar): ("a", chain_a)}[id(eng)]
            links[k] += 1
            ins.then_inc(s, 1)
            eng.wait_ge(s, links[k])

        def chunk_count(n):
            return 16 * sum(W_DMAS[CHUNKS[m][1]] for m in range(n % NW, n + 1, NW))

        def meet(eng):
            meetings[id(eng)] = meetings.get(id(eng), 0) + 1
            eng.drain().then_inc(met, 1)
            eng.wait_ge(met, 3 * meetings[id(eng)])

        u_in = [sem(f"u{i}_in") for i in range(RU)]
        v_in = [sem(f"v{i}_in") for i in range(RV)]
        dots_done, gelu_done, wts_done = sem("dots_done"), sem("gelu_done"), sem("weights_done")
        diag_done, sums_done = sem("diagonals_done"), sem("sums_done")
        acc_read = Signal("acc_read", tiles)
        y_ready = Signal("y_ready", tiles)

        def w_in_weight(t):
            return 0 if t == 1 else W_IN

        handovers = {}

        class Experts:

            def __init__(self, name, slot, lag):
                self.slot, self.lag, self.done, self.n = slot, lag, 0, 0
                self.log = handovers[name] = []

            def front(self, t):
                self.t, self.weight = t, 0

            def share(self, w):
                if self.t == 0:
                    return
                self.weight += w
                self.log.append((self.t, w))
                assert self.weight <= SHARES[self.t], (self.t, self.weight)
                until = BASE[self.t - 1] + SLOTS[self.t - 1] * self.weight // SHARES[self.t] - self.lag
                while self.n < until:
                    self.slot(self.t - 1, self.n)
                    self.n += 1

            def rest(self, t):
                while self.n < BASE[t] + SLOTS[t]:
                    self.slot(t, self.n)
                    self.n += 1

        block = ctx.enter_context(nc.Block())

        T = nc.tensor
        V = nc.vector
        A = nc.scalar

        def mm(o, l, r, start=True, stop=True):
            return T.matmul(o, lhsT=l, rhs=r, start=start, stop=stop, skip_group_check=True)

        def tr(o, i):
            return T.transpose(o, i, ident[0:i.shape[0], 0:i.shape[0]])

        @block.tensor
        def _(pe):
            pe.wait_ge(first_in, FIRST_IN)

            def set_up():
                pe.wait_ge(consts_in, CONSTS_IN)
                pe.wait_ge(setup_in, SETUP_IN)
                for c in range(4):
                    b = take(pe, ("keys", c))
                    for j in range(4):
                        i = tr(b[:, j * 128:(j + 1) * 128], keys_nat[:, 4 * c + j, :])
                    full(i, ("keys", c))
                for c in range(2):
                    b = take(pe, ("uk", c))
                    for r in range(HR):
                        i = tr(b[:, r * 128:(r + 1) * 128], uk_nat[:, c, r * 128:(r + 1) * 128])
                    full(i, ("uk", c))
                relb_ready.wait(pe, 0)
                for h in range(NH):
                    b = take(pe, ("bias_d", h))
                    full(mm(b[:, 0:WD], relb_x[:, h, :], hot_u[:, GU - 384:GU - 384 + WD]), ("bias_d", h))
                for c in range(3):
                    w = min(512, WS - 512 * c)
                    b = take(pe, ("bias_s", c))
                    full(mm(b[0:32, 0:w], relb_s[:, :, :].rearrange("p h t -> p (h t)"), hot_u[:, c * 512:c * 512 + w]),
                         ("bias_s", c))

            def sum_slot(t, n):
                m = P[t]
                if n == BASE[t]:
                    if t:
                        acc_read.wait(pe, t - 1)
                    for c in range(2):
                        mm(acc[0:m, c * 512:(c + 1) * 512], ident[0:m, 0:m], x[t][0:m, c * 512:(c + 1) * 512], True, False)
                pe.wait_ge(diag_done, n + 1)
                pe.wait_ge(v_in[n % RV], (n // RV + 1) * 16)
                for c in range(2):
                    i = mm(acc[0:m, c * 512:c * 512 + 512], d_ring[n % RD][:, 0:m],
                           v_ring[n % RV][:, c * 512:c * 512 + 512], False, False)
                i.then_inc(sums_done, 1)

            experts = Experts("PE", sum_slot, 2)
            share = experts.share

            def transpose_x(t, what):
                for c in range(2):
                    b = take(pe, (what, t, c))
                    src = z if what == "x" else xn2[t]
                    for j in range(4):
                        k = 4 * c + j
                        i = tr(b[:, j * P[t]:(j + 1) * P[t]], src[0:P[t], k * 128:(k + 1) * 128])
                    full(i, (what, t, c))

            def chunk_wait(key):
                n = CHUNKS.index(key)
                pe.wait_ge(w_in_slot[n % NW], chunk_count(n))
                return wring[n % NW]

            def heads_part(t):
                n, r0 = P[t], ROW0[t]
                post_ready.wait(pe, t)
                b = take(pe, ("cq", t))
                for j in range(3):
                    i = tr(b[:, j * n:(j + 1) * n], cqn[0:n, j * 128:(j + 1) * 128])
                full(i, ("cq", t))
                b = take(pe, ("kv", t))
                for j in range(2):
                    tr(b[:, j * 128:j * 128 + n], ckv_nat[0:n, t, j * 128:(j + 1) * 128])
                tr(b[0:QKD, 256:256 + n], kk[0:n, :])
                full(tr(b[:, 384:384 + n], z[0:n, O_KB:O_KB + 128]), ("kv", t))
                b = take(pe, ("qb", t))
                for r in range(HR):
                    i = tr(b[:, r * n:(r + 1) * n], qb_pairs[0:n, r * 128:(r + 1) * 128])
                full(i, ("qb", t))
                share(W_HEADS)
                read_done(pe, ("cq", t))
                for c in range(2):
                    b = take(pe, ("q", t, c))
                    for k in range(3):
                        i = mm(b[0:n, 0:384], cq_t[:, k, 0:n], w_uq[:, k, c * 384:(c + 1) * 384], k == 0, k == 2)
                    full(i, ("q", t, c))
                share(W_HEADS)
                qrope_ready.wait(pe, t)
                b = take(pe, ("qn", t))
                for r in range(HR):
                    i = tr(b[:, r * n:(r + 1) * n], q_nope[0:n, r * 128:(r + 1) * 128])
                full(i, ("qn", t))
                for c in range(2):
                    b = take(pe, ("qq", t, c))
                    for j in range(4):
                        i = tr(b[0:QKD, j * n:(j + 1) * n], qq[0:n, 4 * c + j, :])
                    full(i, ("qq", t, c))
                share(W_HEADS)
                read_done(pe, ("qn", t))
                for u in range(4):
                    b = take(pe, ("ql", t, u))
                    q, j = u // 2, u % 2
                    for m in range(2):
                        for c in range(2):
                            i = mm(b[:, (2 * c + m) * n:(2 * c + m + 1) * n],
                                   uk_t[j * 64:j * 64 + 64, 2 * q + m, c * 128:(c + 1) * 128],
                                   qn_t[j * 64:j * 64 + 64, 2 * q + m, 0:n])
                    full(i, ("ql", t, u))
                share(W_HEADS)

            def values_up(t):
                n = P[t]
                b = take(pe, ("uv", t))
                for h in range(NH):
                    for c in range(2):
                        i = mm(b[(h % 2) * 64:(h % 2) * 64 + 64, (h // 2) * n:(h // 2 + 1) * n],
                               w_uv[:, c, h * VD:(h + 1) * VD], (o_t if t < 2 else o_s)[:, c, h, 0:n], c == 0, c == 1)
                full(i, ("uv", t))

            def prompt(t):
                nk = 128 * (t + 1)
                hp = 512 // nk
                read_done(pe, ("qq", t, 1))
                read_done(pe, ("kv", t))
                for g in range(HG[t]):
                    b = take(pe, ("idx", t, g))
                    for j in range(hp):
                        i = mm(b[:, j * nk:(j + 1) * nk], qq_t[0:IDX, g * hp + j, :], kk_t[0:IDX, 0:nk])
                    full(i, ("idx", t, g))
                    share(1)
                for r in range(TOPK_P // 8):
                    share(1)
                read_done(pe, ("ql", t, 3))

                def logits(kind, g):
                    b = take(pe, (kind, t, g))
                    for j in range(hp):
                        h, o = g * hp + j, b[:, j * nk:(j + 1) * nk]
                        if kind == "m":
                            mm(o, ql_t[:, 0, h, :], ckv_t[:, 0, 0:nk], True, False)
                            mm(o, ql_t[:, 1, h, :], ckv_t[:, 1, 0:nk], False, False)
                            i = mm(o, qq_t[IDX:QKD, h, :], kk_t[IDX:QKD, 0:nk], False, True)
                        else:
                            g2 = h // HR
                            mm(o, qb_t[g2 * 64:g2 * 64 + 64, h % HR, :], kb_t[g2 * 64:g2 * 64 + 64, 0:nk], True, False)
                            i = mm(o, ident[:, :], iscore[:, 0:nk], False, True)
                    full(i, (kind, t, g))

                def probs(kind, g):
                    probs_ready.wait(pe, (kind, t, g))
                    b = take(pe, (kind + "pt", t, g))
                    for j in range(4):
                        i = tr(b[:, j * 128:(j + 1) * 128], s_b[g % 2][:, j * 128:(j + 1) * 128])
                    full(i, (kind + "pt", t, g))

                for g in range(HG[t] + 1):
                    if g:
                        probs("m", g - 1)
                    if g < HG[t]:
                        logits("m", g)
                    if g:
                        read_done(pe, ("mpt", t, g - 1))
                        for c in range(2):
                            b = take(pe, ("ol", t, g - 1, c))
                            for j in range(hp):
                                for k in range(t + 1):
                                    i = mm(b[:, j * 128:(j + 1) * 128], ckv_nat[:, k, c * 128:(c + 1) * 128],
                                           p_t[(g - 1) % 2][:, (j * (t + 1) + k) * 128:(j * (t + 1) + k + 1) * 128],
                                           k == 0, k == t)
                            full(i, ("ol", t, g - 1, c))
                    share(W_PROMPT)
                read_done(pe, ("ol", t, HG[t] - 1, 1))
                values_up(t)
                sel_ready.wait(pe, t)
                for g in range(HG[t] + 1):
                    if g:
                        probs("d", g - 1)
                    if g < HG[t]:
                        logits("d", g)
                    if g:
                        read_done(pe, ("dpt", t, g - 1))
                        b = take(pe, ("od", t, g - 1))
                        for j in range(hp):
                            h = (g - 1) * hp + j
                            for k in range(t + 1):
                                i = mm(b[(h // HR) * 64:(h // HR) * 64 + 64, j * 128:(j + 1) * 128],
                                       v_nat[:, k, (h // HR) * 64:(h // HR) * 64 + 64],
                                       p_t[(g - 1) % 2][:, (j * (t + 1) + k) * 128:(j * (t + 1) + k + 1) * 128],
                                       k == 0, k == t)
                        full(i, ("od", t, g - 1))
                    share(W_PROMPT)

            def sample():
                r0 = ROW0[2]
                new = slice(r0, r0 + 32)

                def transposed(kind, b):
                    if kind == "m":
                        pe.wait_ge(lat_in[b % 3], 32 * (b // 3 + 1) * NPG)
                        for p in range(0, NPG, 2):
                            k = take(pe, ("pc", b, p))
                            for c in range(2):
                                for q in range(2):
                                    i = tr(k[:, (2 * c + q) * 128:(2 * c + q + 1) * 128],
                                           nat_c[b % 3][:, p + q, c * 128:(c + 1) * 128])
                            full(i, ("pc", b, p))
                        for c in range(2):
                            k = take(pe, ("pr", b, c))
                            for q in range(4):
                                i = mm(k[IDX:QKD, q * 128:(q + 1) * 128], nat_r[b % 3][:, 4 * c + q, :], ident[:, :])
                            full(i, ("pr", b, c))
                    else:
                        if kind == "i":
                            pe.wait_ge(idx_in[b], 16 * NPG)
                        else:
                            pe.wait_ge(kv_in[b % 3], 32 * (b // 3 + 1) * NPG)
                        for c in range(2):
                            k = take(pe, ("p" + kind, b, c))
                            for q in range(4):
                                nat = nat_i[b] if kind == "i" else nat_k[b % 3]
                                i = tr(k[0:nat.shape[2], q * 128:(q + 1) * 128], nat[:, 4 * c + q, :])
                            full(i, ("p" + kind, b, c))

                def logits(kind, b):
                    if kind == "m":
                        read_done(pe, ("pc", b, NPG - 2))
                        read_done(pe, ("pr", b, 1))
                    else:
                        read_done(pe, ("pd", b, 1))
                    for u, (c0, w) in enumerate(UC):
                        k = take(pe, (kind + "s", b, u))
                        if kind == "m":
                            keys = ckp_t[:, :, c0:c0 + w] if u < 2 else ckv_t[:, :, new]
                            kr = kr_t[IDX:QKD, c0:c0 + w] if u < 2 else kk_t[IDX:QKD, new]
                            mm(k[0:32, 0:w], ql_s[:, 0, b, :], keys[:, 0, :], True, False)
                            mm(k[0:32, 0:w], ql_s[:, 1, b, :], keys[:, 1, :], False, False)
                            i = mm(k[0:32, 0:w], qq_s[IDX:QKD, b, :], kr, False, True)
                        else:
                            keys = ckp_t[:, b % 2, c0:c0 + w] if u < 2 else kb_t[:, new]
                            mm(k[0:32, 0:w], qblk[:, b, :], keys, True, False)
                            i = mm(k[0:32, 0:w], rep[:, b, :], i_s[:, c0:c0 + w], False, True)
                        full(i, (kind + "s", b, u))

                def turn(kind, b):
                    probs_ready.wait(pe, (kind, b))
                    k = take(pe, (kind + "spt", b))
                    s = s_s[b % 2]
                    for p in range(NPG):
                        tr(k[:, p * 32:(p + 1) * 32], s[:, p * 128:(p + 1) * 128])
                    full(tr(k[0:32, 256:288], s[:, PAST:SK]), (kind + "spt", b))

                def attend(kind, b):
                    read_done(pe, (kind + "spt", b))
                    k = take(pe, (kind + "so", b))
                    nat = (nat_c if kind == "m" else nat_v)[b % 3]
                    own = ckv_nat if kind == "m" else v_nat
                    for c in range(2 if kind == "m" else 1):
                        for p in range(NPG):
                            mm(k[:, c * 32:(c + 1) * 32], nat[:, p, c * 128:(c + 1) * 128], pt_s[:, p, :], p == 0, False)
                        i = mm(k[:, c * 32:(c + 1) * 32], own[0:32, 2, c * 128:(c + 1) * 128], pt_s[0:32, NPG, :], False, True)
                    full(i, (kind + "so", b))

                wexp_ready.wait(pe, 0)
                k = take(pe, ("wcol",))
                for b in range(NB):
                    i = mm(k[0:32, b:b + 1], wexp[:, b, :], ones[:, :])
                full(i, ("wcol",))
                read_done(pe, ("ql", 2, 3))
                read_done(pe, ("qq", 2, 1))
                transposed("i", 0)
                for b in range(NB + 1):
                    if b < NB - 1:
                        transposed("i", b + 1)
                    if b < NB:
                        read_done(pe, ("pi", b, 1))
                        for u, (c0, w) in enumerate(UC):
                            k = take(pe, ("is", b, u))
                            ki = ki_t[b % 2][:, c0:c0 + w] if u < 2 else kk_t[0:IDX, new]
                            full(mm(k[0:32, 0:w], qq_s[0:IDX, b, :], ki), ("is", b, u))
                    if b:
                        read_done(pe, ("is", b - 1, 2))
                        for u, (c0, w) in enumerate(UC):
                            k = take(pe, ("ir", b - 1, u))
                            full(mm(k[0:32, 0:w], rowsum[:, b - 1, :], s_s[(b - 1) % 2][:, c0:c0 + w]), ("ir", b - 1, u))
                    share(2)
                for kind in "md":
                    if kind == "d":
                        sel_ready.wait(pe, 2)
                    transposed(kind, 0)
                    logits(kind, 0)
                    for b in range(NB):
                        if b < NB - 1:
                            transposed(kind, b + 1)
                        share(W_MID[kind])
                        turn(kind, b)
                        if b < NB - 1:
                            logits(kind, b + 1)
                        attend(kind, b)
                        share(W_MID[kind])
                    if kind == "m":
                        read_done(pe, ("mso", NB - 1))
                        values_up(2)

            def product(kind, c, t, width):
                rows_t = xt[t] if kind == "z" else mix_t[t]
                b = take(pe, (kind, c, t))
                for half in range(2):
                    key = (t, "in" if kind == "z" else "out", 2 * c + half)
                    w, m = chunk_wait(key), min(CW, width - CW * half)
                    for k in range(8):
                        i = mm(b[0:P[t], CW * half:CW * half + m], rows_t[:, k, 0:P[t]], w[:, k, 0:m], k == 0, k == 7)
                    if half == 0:
                        w_even_used.send(i, key)
                        share(w_in_weight(t) if kind == "z" else W_IN)
                full(i, (kind, c, t))

            for t in tiles:
                n = P[t]
                experts.front(t)
                meet(pe)
                xn_ready.wait(pe, t)
                transpose_x(t, "x")
                share(w_in_weight(t))
                read_done(pe, ("x", t, 1))
                for c in range(4):
                    product("z", c, t, ZC[c])
                    share(w_in_weight(t))
                meet(pe)
                if t == 0:
                    set_up()
                heads_part(t)
                if t < 2:
                    prompt(t)
                else:
                    meet(pe)
                    sample()
                meet(pe)
                for c in range(2):
                    product("wo", c, t, 512)
                    share(W_IN)
                xn2_ready.wait(pe, t)
                transpose_x(t, "x2")
                share(W_IN)
                read_done(pe, ("x2", t, 1))
                for c in range(4):
                    b = take(pe, ("pq", c, t))
                    for half in range(2):
                        w = chunk_wait((t, "pq", 2 * c + half))
                        for j in range(2):
                            q = 2 * half + j
                            for k in range(8):
                                i = mm(b[:, q * n:(q + 1) * n], w[:, k, j * 128:(j + 1) * 128], xt[t][:, k, 0:n],
                                       k == 0, k == 7)
                        if half == 0:
                            w_even_used.send(i, (t, "pq", 2 * c))
                            share(W_PQ)
                    full(i, ("pq", c, t))
                    share(W_PQ)
                    read_done(pe, ("pq", c, t))
                    b = take(pe, ("sc", c, t))
                    for j in range(4):
                        i = mm(b[0:n, j * 128:(j + 1) * 128], qp_t[c % 2][:, j, 0:n], keys_t[:, 4 * c + j, :])
                    full(i, ("sc", c, t))
                for w in CHOOSE:
                    share(w)
                if t:
                    experts.rest(t - 1)
            experts.rest(2)

        @block.scalar
        def _(act):
            def copy(name, o, i, last=True):
                c = A.activation(o, i, ACT.Copy)
                if last:
                    drained(c, name)

            def set_up():
                for c in range(4):
                    b = ready(act, ("keys", c))
                    copy(("keys", c), keys_t[:, 4 * c:4 * c + 4, :], b[:, :].rearrange("p (a b) -> p a b", b=128))
                for c in range(2):
                    b = ready(act, ("uk", c))
                    copy(("uk", c), uk_t[:, :, c * 128:(c + 1) * 128], b[:, :].rearrange("p (a b) -> p a b", b=128))
                for h in range(NH):
                    b = ready(act, ("bias_d", h))
                    copy(("bias_d", h), gd[:, h, :], b[:, 0:WD])
                for c in range(3):
                    w = min(512, WS - 512 * c)
                    b = ready(act, ("bias_s", c))
                    copy(("bias_s", c), gs[:, c * 512:c * 512 + w], b[0:32, 0:w])

            def weigh_slot(t, n):
                k = n % RC
                act.wait_ge(dots_done, n + 1)
                A.activation(gelus[:, k:k + 1], dots[:, k:k + 1], ACT.Gelu).then_inc(gelu_done, 1)
                act.wait_ge(gelu_done, n + 1)
                j = n - BASE[t]
                A.activation(wts[:, k:k + 1], gelus[:, k:k + 1], ACT.Copy, scale=gate[t][:, j:j + 1]).then_inc(wts_done, 1)
                act.wait_ge(wts_done, n + 1)
                if n >= RD:
                    act.wait_ge(sums_done, n - RD + 1)
                m = P[t]
                A.activation(d_ring[n % RD][:, 0:m], (ident if t < 2 else sel_sample)[:, 0:m], ACT.Copy,
                             scale=wts[:, k:k + 1]).then_inc(diag_done, 1)

            experts = Experts("Activation", weigh_slot, 1)
            share = experts.share

            def root(step, cols=slice(4, 5)):
                s = small[0:P[step[1]], cols]
                square_ready.wait(act, step)
                root_ready.send(A.activation(s, s, ACT.Sqrt), step)

            def split(a, m, n):
                return a.rearrange("p (a b) -> p a b", a=m)[:, :, 0:n]

            def x_evac(what, t):
                for c in range(2):
                    b = ready(act, (what, t, c))
                    copy((what, t, c), xt[t][:, 4 * c:4 * c + 4, :], split(b[:, 0:4 * P[t]], 4, P[t]))

            def heads_part(t):
                n, r0 = P[t], ROW0[t]
                b = ready(act, ("cq", t))
                copy(("cq", t), cq_t[:, :, 0:n], split(b[:, 0:3 * n], 3, n))
                b = ready(act, ("kv", t))
                copy(None, ckv_t[:, :, r0:r0 + n], split(b[:, 0:256], 2, n), False)
                copy(None, kk_t[:, r0:r0 + n], b[0:QKD, 256:256 + n], False)
                copy(("kv", t), kb_t[:, r0:r0 + n], b[:, 384:384 + n])
                b = ready(act, ("qb", t))
                copy(("qb", t), qb_t[:, :, 0:n], split(b[:, 0:4 * n], 4, n))
                share(W_HEADS)
                for c in range(2):
                    b = ready(act, ("q", t, c))
                    heads = b[0:n, 0:384].rearrange("p (h d) -> p h d", d=QKD)
                    copy(None, q_nope[0:n, c * 256:(c + 1) * 256].rearrange("p (h d) -> p h d", d=NOPE),
                         heads[:, :, 0:NOPE], False)
                    copy(("q", t, c), q_rope[0:n, c * 128:(c + 1) * 128].rearrange("p (h d) -> p h d", d=ROPE),
                         heads[:, :, NOPE:QKD])
                share(W_HEADS)
                b = ready(act, ("qn", t))
                copy(("qn", t), qn_t[:, :, 0:n], split(b[:, 0:4 * n], 4, n))
                for c in range(2):
                    b = ready(act, ("qq", t, c))
                    if t < 2:
                        copy(("qq", t, c), qq_t[:, 4 * c:4 * c + 4, 0:n], split(b[0:QKD, 0:4 * n], 4, n))
                    else:
                        copy(("qq", t, c), free(qq_s[:, 0, 16 * c:16 * c + 1], (NT, 4), (32, NB), (1, NT)),
                             free(b[0:QKD, 0:1], (32, 4), (NT, NB), (1, NT)))
                share(W_HEADS)
                for u in range(4):
                    b = ready(act, ("ql", t, u))
                    h = 4 * (u // 2) + u % 2
                    if t < 2:
                        copy(("ql", t, u), ql_t[:, :, h:h + 3:2, 0:n],
                             b[:, 0:4 * n].rearrange("p (c j n) -> p c j n", c=2, j=2))
                    else:
                        for c in range(2):
                            copy(("ql", t, u), free(ql_s[:, c, 0, NT * h:NT * h + 1], (2 * NT, 2), (32, NB), (1, NT)),
                                 free(b[:, 64 * c:64 * c + 1], (32, 2), (NT, NB), (1, NT)), c == 1)
                share(W_HEADS)

            def prompt(t):
                nk = 128 * (t + 1)
                hp = 512 // nk
                steps = [(k, g) for k in "md" for g in range(HG[t])]
                for g in range(HG[t]):
                    b = ready(act, ("idx", t, g))
                    if g >= 2:
                        relu_used.wait(act, (t, g - 2))
                    drained(A.activation(relu[g % 2][:, :], b[:, :], ACT.Relu), ("idx", t, g))
                    share(1)
                for r in range(TOPK_P // 8):
                    share(1)
                act.wait_ge(stored_z, 80 * (t + 1))

                def exps(kind, g):
                    logits_sb.wait(act, (kind, t, g))
                    for j in range(hp):
                        s = s_b[g % 2][:, j * nk:(j + 1) * nk]
                        i = A.activation(s, s, ACT.Exp, bias=small[:, 32 + 8 * (g % 2) + j:33 + 8 * (g % 2) + j],
                                         accum_out=small[:, 48 + 8 * (g % 2) + j:49 + 8 * (g % 2) + j])
                    exps_ready.send(i, (kind, t, g))

                def turned(kind, g):
                    b = ready(act, (kind + "pt", t, g))
                    n = steps.index((kind, g))
                    if n >= 2:
                        k2, g2 = steps[n - 2]
                        ready(act, ("ol", t, g2, 1) if k2 == "m" else ("od", t, g2))
                    copy((kind + "pt", t, g), p_t[g % 2][:, :], b[:, :])

                def outputs(kind, g):
                    if kind == "m":
                        for c in range(2):
                            b = ready(act, ("ol", t, g, c))
                            copy(("ol", t, g, c), o_t[:, c, g * hp:(g + 1) * hp, :],
                                 b[:, 0:hp * 128].rearrange("p (a b) -> p a b", b=128))
                    else:
                        b = ready(act, ("od", t, g))
                        g2, r = g * hp // HR, g * hp % HR
                        copy(("od", t, g), mix_t[t][g2 * 64:g2 * 64 + 64, 4 + r:4 + r + hp, :],
                             b[g2 * 64:g2 * 64 + 64, 0:hp * 128].rearrange("p (a b) -> p a b", b=128))

                for kind in "md":
                    for g in range(HG[t] + 1):
                        if g:
                            turned(kind, g - 1)
                        if g < HG[t]:
                            exps(kind, g)
                        if g:
                            outputs(kind, g - 1)
                        share(W_PROMPT)
                    if kind == "m":
                        b = ready(act, ("uv", t))
                        copy(("uv", t), mix_t[t][:, 0:4, :], b[:, :].rearrange("p (a b) -> p a b", b=128))

            def sample():
                b_ = ready(act, ("wcol",))
                copy(("wcol",), wcol[:, :], b_[0:32, 0:NB])

                def evacuate(kind, b):
                    if kind == "m":
                        for p in range(0, NPG, 2):
                            k = ready(act, ("pc", b, p))
                            if p == 0:
                                ready(act, ("ms", b - 1, 1) if b else ("is", NB - 1, 1))
                            copy(("pc", b, p), ckp_t[:, :, p * 128:(p + 2) * 128], split(k[:, :], 2, 256))
                        for c in range(2):
                            k = ready(act, ("pr", b, c))
                            copy(("pr", b, c), kr_t[IDX:QKD, c * 512:(c + 1) * 512], k[IDX:QKD, :])
                    else:
                        for c in range(2):
                            k = ready(act, ("p" + kind, b, c))
                            if c == 0:
                                if b > 1:
                                    ready(act, (kind + "s", b - 2, 1))
                                elif kind == "d":
                                    ready(act, ("ms", NB - 1, 1))
                            o = ki_t[b % 2] if kind == "i" else ckp_t[:, b % 2, :]
                            copy(("p" + kind, b, c), o[:, c * 512:(c + 1) * 512], k[0:o.shape[0], :])

                def exps(kind, b):
                    logits_sb.wait(act, (kind, b))
                    s, c = s_s[b % 2], 8 * (b % 2)
                    exps_ready.send(A.activation(s, s, ACT.Exp, bias=small[0:32, 32 + c:33 + c],
                                                 accum_out=small[0:32, 48 + c:49 + c]), (kind, b))

                def outputs(kind, b):
                    k = ready(act, (kind + "spt", b))
                    copy(None, pt_s[:, 0:NPG, :], k[:, 0:256].rearrange("p (a b) -> p a b", b=32), False)
                    copy((kind + "spt", b), pt_s[0:32, NPG, :], k[0:32, 256:288])
                    k = ready(act, (kind + "so", b))
                    qr = slice(NT * b, NT * b + NT)
                    for c in range(2):
                        if kind == "m":
                            i = A.activation(o_s[:, c, :, qr], k[:, c * 32:(c + 1) * 32].rearrange("p (h t) -> p h t", h=NH),
                                             ACT.Copy)
                        else:
                            half = slice(c * 64, c * 64 + 64)
                            i = A.activation(mix_t[2][half, 4:8, qr],
                                             k[half, c * 16:c * 16 + 16].rearrange("p (h t) -> p h t", h=HR), ACT.Copy)
                        if c == 0:
                            (lat_used if kind == "m" else kv_used).send(i, b)
                    drained(i, (kind + "so", b))

                evacuate("i", 0)
                for b in range(NB + 1):
                    if b < NB - 1:
                        evacuate("i", b + 1)
                    share(2)
                for kind in "md":
                    evacuate(kind, 0)
                    exps(kind, 0)
                    for b in range(NB):
                        if b < NB - 1:
                            evacuate(kind, b + 1)
                        share(W_MID[kind])
                        outputs(kind, b)
                        if b < NB - 1:
                            exps(kind, b + 1)
                        share(W_MID[kind])
                    if kind == "m":
                        k = ready(act, ("uv", 2))
                        copy(("uv", 2), mix_t[2][:, 0:4, :], split(k[:, 0:128], 4, 32))

            def gate_exps(t):
                n = P[t]
                gate_sub.wait(act, t)
                gate_exp.send(A.activation(gt[0:n, :, :], gt[0:n, :, :], ACT.Exp), t)

            for t in tiles:
                n = P[t]
                experts.front(t)
                meet(act)
                root(("x", t))
                x_evac("x", t)
                share(w_in_weight(t))
                for c in range(4):
                    share(w_in_weight(t))
                    b = ready(act, ("z", c, t))
                    copy(("z", c, t), z[0:n, c * 512:c * 512 + ZC[c]], b[0:n, 0:ZC[c]])
                    share(w_in_weight(t))
                if t == 1:
                    gate_exps(0)
                meet(act)
                root(("z", t), slice(0, 2))
                if t == 0:
                    set_up()
                heads_part(t)
                if t < 2:
                    prompt(t)
                else:
                    act.wait_ge(stored_z, 80 * (t + 1))
                    meet(act)
                    sample()
                meet(act)
                for c in range(2):
                    share(W_IN)
                    share(W_IN)
                root(("h", t))
                x_evac("x2", t)
                share(W_IN)
                for c in range(4):
                    share(W_PQ)
                    b = ready(act, ("pq", c, t))
                    if c > 1:
                        ready(act, ("sc", c - 2, t))
                    copy(("pq", c, t), qp_t[c % 2][:, :, 0:n], split(b[:, 0:4 * n], 4, n))
                    share(W_PQ)
                for i, w in enumerate(CHOOSE):
                    if i == 4 and t:
                        gate_exps(t)
                    share(w)
                if t:
                    experts.rest(t - 1)
                    root(("y", t - 1))
            experts.rest(2)
            root(("y", 2))

        @block.vector
        def _(dve):
            def dot_slot(t, n):
                k = n % RC
                dve.wait_ge(u_in[n % RU], (n // RU + 1) * 16)
                if n >= RC:
                    dve.wait_ge(gelu_done, n - RC + 1)
                V.tensor_tensor_reduce(out=u_ring[n % RU], in0=u_ring[n % RU], in1=xn2[t][:, :], scale=1.0, scalar=0.0,
                                       op0=ALU.mult, op1=ALU.add, accum_out=dots[:, k:k + 1]).then_inc(dots_done, 1)

            experts = Experts("DVE", dot_slot, 0)
            share = experts.share

            def mean_square(src, width, col, junk):
                n = src.shape[0]
                a = small[0:n, col:col + 1]
                link(V, V.tensor_tensor_reduce(out=junk, in0=src, in1=src, scale=1.0, scalar=0.0, op0=ALU.mult,
                                               op1=ALU.add, accum_out=a))
                return V.tensor_scalar(a, a, 1.0 / width, EPS, ALU.mult, ALU.add)

            def norm(src, gain, o, col):
                a = small[0:src.shape[0], col:col + 1]
                return V.scalar_tensor_tensor(out=o, in0=src, scalar=a, in1=gain, op0=ALU.mult, op1=ALU.mult)

            def rms(src, gain, o, step, sig, t):
                square_ready.send(mean_square(src, DM, 4, o), step)
                root_ready.wait(dve, step)
                a = small[0:src.shape[0], 4:5]
                link(V, V.reciprocal(a, a))
                sig.send(norm(src, gain, o, 4), t)
                sig.wait(dve, t)

            def rope(t, src, heads, stride, o, o_stride):
                n = P[t]
                cc = free(ropet[0:n, t, 0:1], (0, heads), (1, 32))
                for half in range(2):
                    other = src.offset + 16 * (1 - half)
                    V.tensor_tensor(rope_b[0:n, 0:heads, 16 * half:16 * half + 16],
                                    bass.AP(src.tensor, other, [list(src.ap[0]), [stride, heads], [1, 16]]),
                                    free(ropet[0:n, t, 32 + 16 * half:33 + 16 * half], (0, heads), (1, 16)), ALU.mult)
                link(V, V.tensor_tensor(rope_a[0:n, 0:heads, :], free(src, (stride, heads), (1, 32)), cc, ALU.mult))
                return V.tensor_tensor(free(o, (o_stride, heads), (1, 32)), rope_a[0:n, 0:heads, :],
                                       rope_b[0:n, 0:heads, :], ALU.add)

            def post(t):
                n, zt = P[t], z
                if t == 0:
                    dve.wait_ge(setup_in, SETUP_IN)
                    V.tensor_copy(relb_x[:, :, :], free(relb[:, 0:1], (1, NH), (0, 128)))
                    relb_ready.send(V.tensor_copy(relb_s[:, :, :], free(relb[:, 0:1], (1, NH), (0, NT))), 0)
                    dve.wait_ge(consts_in, CONSTS_IN)
                read_done(dve, ("z", 3, t))
                link(V, V.tensor_copy(v_nat[0:n, t, :], zt[0:n, O_VB:O_VB + 128]))
                z_q, z_kv = zt[0:n, O_CQ:O_CQ + QL], zt[0:n, O_CKV:O_CKV + KVL]
                mean_square(z_q, QL, 0, cqn[0:n, :])
                square_ready.send(mean_square(z_kv, KVL, 1, ckv_nat[0:n, t, :]), ("z", t))
                root_ready.wait(dve, ("z", t))
                link(V, V.reciprocal(small[0:n, 0:2], small[0:n, 0:2]))
                norm(z_q, g_q[0:n, :], cqn[0:n, :], 0)
                norm(z_kv, g_kv[0:n, :], ckv_nat[0:n, t, :], 1)
                link(V, rope(t, zt[0:n, O_KR:O_KR + 1], 1, 32, kk[0:n, IDX:IDX + 1], 32))
                link(V, rope(t, zt[0:n, O_KI:O_KI + 1], 1, 32, kk[0:n, 0:1], 32))
                V.tensor_copy(kk[0:n, 32:IDX], zt[0:n, O_KI + 32:O_KI + IDX])
                V.tensor_scalar(small[0:n, 16:24], zt[0:n, O_WI:O_WI + NH], IDX_W, None, ALU.mult)
                for r in range(HR):
                    V.tensor_copy(free(qb_pairs[0:n, r * 128:r * 128 + 1], (64, 2), (1, 64)),
                                  free(zt[0:n, O_QB + r * HD:O_QB + r * HD + 1], (HR * HD, 2), (1, HD)))
                link(V, rope(t, zt[0:n, O_QI:O_QI + 1], NH, IDX, qq[0:n, 0, 0:1], QKD))
                post_ready.send(V.tensor_copy(qq[0:n, :, 32:IDX],
                                              free(zt[0:n, O_QI + 32:O_QI + 33], (IDX, NH), (1, 32))), t)
                post_ready.wait(dve, t)
                share(W_HEADS)
                read_done(dve, ("q", t, 1))
                qrope_ready.send(rope(t, q_rope[0:n, 0:1], NH, ROPE, qq[0:n, 0, IDX:IDX + 1], QKD), t)
                for i in range(3):
                    share(W_HEADS)

            def normalise(key, s, width, heads, n, c):
                exps_ready.wait(dve, key)
                rec = small[0:n, 64 + c:64 + c + heads]
                link(V, V.reciprocal(rec, small[0:n, 48 + c:48 + c + heads]))
                if heads == 1:
                    i = V.tensor_scalar(s, s, rec, None, ALU.mult)
                else:
                    v = s.rearrange("p (a b) -> p a b", a=heads)
                    i = V.tensor_tensor(v, v, free(rec, (1, heads), (0, width)), ALU.mult)
                probs_ready.send(i, key)

            def prompt(t):
                nk = 128 * (t + 1)
                hp = 512 // nk
                mask = tri[:, 256 - nk:256]
                first = mask
                for g in range(HG[t]):
                    read_done(dve, ("idx", t, g))
                    for j in range(hp):
                        h = g * hp + j
                        i = V.scalar_tensor_tensor(out=iscore[:, 0:nk], in0=relu[g % 2][:, j * nk:(j + 1) * nk],
                                                   scalar=small[:, 16 + h:17 + h], in1=first, op0=ALU.mult, op1=ALU.add)
                        first = iscore[:, 0:nk]
                        if j < hp - 1:
                            link(V, i)
                        else:
                            relu_used.send(i, (t, g))
                            relu_used.wait(dve, (t, g))
                    share(1)
                src = iscore[:, 0:nk]
                for r in range(TOPK_P // 8):
                    link(V, V.max(small[:, 24:32], src))
                    link(V, V.match_replace(out=iwork[:, 0:nk], in_to_replace=small[:, 24:32], in_values=src,
                                            imm_value=TAKEN))
                    src = iwork[:, 0:nk]
                    share(1)
                link(V, V.tensor_scalar(iscore[:, 0:nk], src, TAKEN, -NEG, ALU.is_equal, ALU.mult))
                sel_ready.send(V.scalar_tensor_tensor(out=iscore[:, 0:nk], in0=iscore[:, 0:nk], scalar=NEG, in1=mask,
                                                      op0=ALU.add, op1=ALU.add), t)
                if t == 0:
                    dve.wait_ge(bias_in, 16 * (NH + 1))
                    V.tensor_copy(free(bias_s[:, PAST + NT:PAST + NT + 1], (NT, NB - 1), (1, NT)),
                                  free(bias_s[:, PAST:PAST + 1], (0, NB - 1), (1, NT)))
                steps = [(k, g) for k in "md" for g in range(HG[t])]

                def logits(kind, g):
                    b = ready(dve, (kind, t, g))
                    n = steps.index((kind, g))
                    if n >= 2:
                        k2, g2 = steps[n - 2]
                        ready(dve, (k2 + "pt", t, g2))
                    s = s_b[g % 2]
                    add = free(mask, (0, hp), (1, nk)) if kind == "m" else bias_d[:, g * hp:(g + 1) * hp, 256 - nk:256]
                    drained(V.scalar_tensor_tensor(
                        out=s.rearrange("p (a b) -> p a b", a=hp), in0=b[:, :].rearrange("p (a b) -> p a b", a=hp),
                        scalar=MLA_SCALE if kind == "m" else DSA_SCALE, in1=add, op0=ALU.mult, op1=ALU.add), (kind, t, g))
                    read_done(dve, (kind, t, g))
                    c = 8 * (g % 2)
                    logits_sb.send(V.tensor_reduce(out=small[:, 32 + c:32 + c + hp],
                                                   in_=s.rearrange("p (a b) -> p a b", a=hp), axis=AX.X, op=ALU.max,
                                                   negate=True), (kind, t, g))

                for kind in "md":
                    for g in range(HG[t] + 1):
                        if g:
                            normalise((kind, t, g - 1), s_b[(g - 1) % 2], nk, hp, 128, 8 * ((g - 1) % 2))
                        if g < HG[t]:
                            logits(kind, g)
                        share(W_PROMPT)

            def sample():
                wexp_ready.send(V.tensor_tensor(free(wexp[:, 0, 0:1], (32, NB), (NT, NH), (1, NT)),
                                                free(small[0:32, 16:17], (0, NB), (1, NH), (0, NT)),
                                                free(rep[:, 0, 0:1], (32, NB), (NT, NH), (1, NT)), ALU.mult), 0)
                link(V, V.memset(qblk[:, :, :], 0.0))
                for g2 in range(KG):
                    q = slice(g2 * 64, g2 * 64 + 64)
                    V.tensor_copy(free(qblk[q, 0, g2 * 16:g2 * 16 + 1], (32, NB), (NT, HR), (1, NT)),
                                  free(qb_t[q, 0, 0:1], (NT, NB), (128, HR), (1, NT)))
                V.memset(i_s[:, 0:PAST], 0.0)
                link(V, V.tensor_copy(i_s[:, PAST:SK], newmask_i[:, :]))
                read_done(dve, ("wcol",))

                def logits(kind, b):
                    s = s_s[b % 2]
                    if b > 1:
                        ready(dve, (kind + "spt", b - 2))
                    elif kind == "d":
                        ready(dve, ("mspt", NB - 2 + b))
                    for u, (c0, w) in enumerate(UC):
                        k = ready(dve, (kind + "s", b, u))
                        o, i = s[:, c0:c0 + w], k[0:32, 0:w]
                        if kind == "d":
                            y = V.scalar_tensor_tensor(out=o, in0=i, scalar=DSA_SCALE, in1=bias_s[:, c0:c0 + w],
                                                       op0=ALU.mult, op1=ALU.add)
                        elif u < 2:
                            y = V.tensor_scalar(o, i, MLA_SCALE, None, ALU.mult)
                        else:
                            y = V.scalar_tensor_tensor(out=o, in0=i, scalar=MLA_SCALE, in1=newmask[:, b, :],
                                                       op0=ALU.mult, op1=ALU.add)
                        drained(y, (kind + "s", b, u))
                    for u in range(3):
                        read_done(dve, (kind + "s", b, u))
                    c = 32 + 8 * (b % 2)
                    logits_sb.send(V.tensor_reduce(out=small[0:32, c:c + 1], in_=s, axis=AX.X, op=ALU.max,
                                                   negate=True), (kind, b))

                for b in range(NB + 1):
                    if b < NB:
                        for u, (c0, w) in enumerate(UC):
                            k = ready(dve, ("is", b, u))
                            drained(V.tensor_scalar(s_s[b % 2][:, c0:c0 + w], k[0:32, 0:w], 0.0, wcol[:, b:b + 1],
                                                    ALU.max, ALU.mult), ("is", b, u))
                    if b:
                        for u, (c0, w) in enumerate(UC):
                            k = ready(dve, ("ir", b - 1, u))
                            drained(V.tensor_tensor(i_s[:, c0:c0 + w], i_s[:, c0:c0 + w], k[0:32, 0:w], ALU.add),
                                    ("ir", b - 1, u))
                        for u in range(3):
                            read_done(dve, ("ir", b - 1, u))
                    share(2)

                def rounds():
                    for r in range(TOPK_S // 8 // NB):
                        link(V, V.max(small[0:32, 24:32], i_s))
                        link(V, V.match_replace(out=i_s, in_to_replace=small[0:32, 24:32], in_values=i_s, imm_value=TAKEN))

                for kind in "md":
                    logits(kind, 0)
                    for b in range(NB):
                        normalise((kind, b), s_s[b % 2], SK, 1, 32, 8 * (b % 2))
                        share(W_MID[kind])
                        if kind == "m":
                            rounds()
                        if b < NB - 1:
                            logits(kind, b + 1)
                        share(W_MID[kind])
                    if kind == "m":
                        link(V, V.tensor_scalar(i_s, i_s, TAKEN, -NEG, ALU.is_equal, ALU.mult))
                        sel_ready.send(V.tensor_scalar(i_s, i_s, NEG, None, ALU.add), 2)

            def top16(score, work, values, index, last=None, pause=lambda: None):
                m = len(score)
                for j in range(m):
                    i = V.max(values[j][:, 0:8], score[j])
                link(V, i)
                pause()
                for j in range(m):
                    V.max_index(index[j][:, 0:8], values[j][:, 0:8], score[j])
                    i = V.match_replace(out=work[j], in_to_replace=values[j][:, 0:8], in_values=score[j], imm_value=TAKEN)
                if last:
                    drained(i, last)
                    read_done(dve, last)
                else:
                    link(V, i)
                pause()
                for j in range(m):
                    i = V.max(values[j][:, 8:16], work[j])
                link(V, i)
                pause()
                for j in range(m):
                    i = V.max_index(index[j][:, 8:16], values[j][:, 8:16], work[j])
                link(V, i)
                pause()

            def choose(t):
                n, cand = P[t], cands[t]
                weights = iter(CHOOSE)

                def pause():
                    if t:
                        share(next(weights))

                link(V, V.tensor_tensor(cand[0:n, :, :].rearrange("p h (a b) -> p h a b", a=16),
                                        free(sv[0:n, 0, 0:1], (32, NH), (1, 16), (0, 16)),
                                        free(sv[0:n, 1, 0:1], (32, NH), (0, 16), (1, 16)), ALU.add))
                hs = range(NH)
                c_ = [cand[0:n, h, :] for h in hs]
                top16(c_, c_, [cv[0:n, h, :] for h in hs], [ci[0:n, h, :] for h in hs],
                      pause=pause)
                gate_sub.send(V.tensor_tensor(gt[0:n, :, :], cv[0:n, :, :], free(cv[0:n, 0, 0:1], (PTOP, NH), (0, PTOP)),
                                              ALU.subtract), t)
                V.tensor_copy(si[0:n, :, :], si_u[0:n, :, :])
                for half, (op, imm, e) in enumerate(((ALU.logical_shift_right, 4, ea), (ALU.bitwise_and, 15, eb))):
                    link(V, V.tensor_scalar(ca[0:n, :, :], ci[0:n, :, :], imm, None, op))
                    link(V, V.tensor_tensor(hot[0:n, :, :], free(ca[0:n, 0, 0:1], (1, NH * PTOP), (0, 16)),
                                            free(iota16[0:n, 0:1], (0, NH * PTOP), (1, 16)), ALU.is_equal))
                    pause()
                    hv = free(hot[0:n, 0, 0:1], (256, NH), (16, PTOP), (1, 16))
                    link(V, V.tensor_tensor(hv, hv, free(si[0:n, half, 0:1], (32, NH), (0, PTOP), (1, 16)), ALU.mult))
                    link(V, V.tensor_reduce(out=e[0:n, :], in_=hot[0:n, :, :], axis=AX.X, op=ALU.add))
                    pause()
                o = eid[t] if t < 2 else eu
                link(V, V.scalar_tensor_tensor(out=o[0:n, :], in0=ea[0:n, :], scalar=float(KEYS), in1=eb[0:n, :],
                                               op0=ALU.mult, op1=ALU.add))
                pause()
                gate_exp.wait(dve, t)
                link(V, V.tensor_reduce(out=small[0:n, 96:104], in_=gt[0:n, :, :], axis=AX.X, op=ALU.add))
                link(V, V.reciprocal(small[0:n, 104:112], small[0:n, 96:104]))
                rc = free(small[0:n, 104:105], (1, NH), (0, PTOP))
                if t < 2:
                    slots_ready.send(V.tensor_tensor(gate[t][0:n, :].rearrange("p (h k) -> p h k", h=NH), gt[0:n, :, :],
                                                     rc, ALU.mult), t)
                else:
                    link(V, V.tensor_tensor(gt[0:n, :, :], gt[0:n, :, :], rc, ALU.mult))
                    gf = gt[0:n, :, :].rearrange("p h k -> p (h k)")
                    for q in range(4):
                        V.tensor_copy(gate[2][q * 32:q * 32 + 32, :], gf[:, q * 32:q * 32 + 32])
                        if q:
                            V.tensor_copy(xn2[2][q * 32:q * 32 + 32, :], xn2[2][0:32, :])
                        i = V.tensor_copy(eid[2][q * 32:q * 32 + 32, :], eu[0:32, q * 32:q * 32 + 32])
                    slots_ready.send(i, t)
                slots_ready.wait(dve, t)

            def finish(t):
                n = P[t]
                dve.wait_ge(sums_done, BASE[t] + SLOTS[t])
                acc_read.send(V.tensor_copy(x[t][0:n, :], acc[0:n, :]), t)
                acc_read.wait(dve, t)
                rms(x[t][0:n, :], g_fin[0:n, :], xn2[t][0:n, :], ("y", t), y_ready, t)

            for t in tiles:
                n = P[t]
                experts.front(t)
                meet(dve)
                dve.wait_ge(x_in[t], 16)
                if t == 0:
                    dve.wait_ge(first_in, FIRST_IN)
                rms(x[t][0:n, :], g_attn[0:n, :], z[0:n, 0:DM], ("x", t), xn_ready, t)
                if t == 1:
                    choose(0)
                share(w_in_weight(t))
                for c in range(4):
                    share(w_in_weight(t))
                    share(w_in_weight(t))
                meet(dve)
                post(t)
                if t < 2:
                    prompt(t)
                else:
                    meet(dve)
                    sample()
                meet(dve)
                for c in range(2):
                    share(W_IN)
                    b = ready(dve, ("wo", c, t))
                    h = x[t][0:n, c * 512:(c + 1) * 512]
                    drained(V.tensor_tensor(h, h, b[0:n, :], ALU.add), ("wo", c, t))
                    share(W_IN)
                for c in range(2):
                    read_done(dve, ("wo", c, t))
                if t == 2:
                    dve.wait_ge(y_out, 16)
                rms(x[t][0:n, :], g_ffn[0:n, :], xn2[t][0:n, :], ("h", t), xn2_ready, t)
                share(W_IN)
                for c in range(4):
                    share(W_PQ)
                    share(W_PQ)
                    b = ready(dve, ("sc", c, t))
                    top16([b[0:n, j * 128:(j + 1) * 128] for j in range(4)], [sc[0:n, j, :] for j in range(4)],
                          [sv[0:n, 4 * c + j, :] for j in range(4)], [si_u[0:n, 4 * c + j, :] for j in range(4)],
                          ("sc", c, t))
                if t:
                    choose(t)
                    experts.rest(t - 1)
                    finish(t - 1)
            experts.rest(2)
            finish(2)
            assert handovers["PE"] == handovers["Activation"] == handovers["DVE"]
            for t in (1, 2):
                assert sum(w for u, w in handovers["DVE"] if u == t) == SHARES[t], (t, sum(w for u, w in handovers["DVE"] if u == t))

        @block.gpsimd
        def _(pool):
            read_done(pool, ("bias_d", NH - 1))
            nc.gpsimd.dma_start(scr_d, gd[:, :, :]).then_inc(scr_d_out, 16)
            read_done(pool, ("bias_s", 2))
            nc.gpsimd.dma_start(scr_s, gs[:, :]).then_inc(scr_s_out, 16)
            pool.wait_ge(scr_d_out, 16)
            nc.gpsimd.dma_start(bias_d[:, :, :], bass.AP(scr_d.tensor, 127, [[NH * WD - 1, 128], [WD, NH], [1, 256]])
                                ).then_inc(bias_in, 16)
            pool.wait_ge(scr_s_out, 16)
            for h in range(NH):
                nc.gpsimd.dma_start(bias_s[h * NT:(h + 1) * NT, 0:PAST + NT],
                                    bass.AP(scr_s.tensor, h * NT * WS + NT - 1, [[WS - 1, NT], [1, PAST + NT]])
                                    ).then_inc(bias_in, 16)
            for t in tiles:
                slots_ready.wait(pool, t)
                for j in range(SLOTS[t]):
                    n = BASE[t] + j
                    if n >= RU:
                        pool.wait_ge(dots_done, n - RU + 1)
                    nc.gpsimd.indirect_dma_start(
                        out=u_ring[n % RU], out_offset=None, in_=inp["peer_u"],
                        in_offset=bass.IndirectOffsetOnAxis(ap=eid[t][:, j:j + 1], axis=0)).then_inc(u_in[n % RU], 16)
                    if n >= RV:
                        pool.wait_ge(sums_done, n - RV + 1)
                    nc.gpsimd.indirect_dma_start(
                        out=v_ring[n % RV], out_offset=None, in_=inp["peer_v"],
                        in_offset=bass.IndirectOffsetOnAxis(ap=eid[t][:, j:j + 1], axis=0)).then_inc(v_in[n % RV], 16)

        @block.sync
        def _(sp):
            def load(o, i, s):
                sp.dma_start(o, i).then_inc(s, 16)

            def bcast(src, n):
                return bass.AP(src.tensor, src.offset, [[0, 128], [1, n]])

            sp.dma_start(x[0][:, :], inp["x_prompt"][0, 0:128, :]).then_inc(x_in[0], 16)
            load(g_attn[:, :], bcast(inp["g_attn"], DM), first_in)
            load(ident[:, :], cst["ident"], first_in)
            early = [(tri[:, :], cst["tri"]), (sel_sample[:, :], cst["sel"]), (iota16[:, :], cst["iota"]),
                     (ropet[:, 0:2, :], cst["rope"][0:256, :].rearrange("(a p) c -> p a c", p=128)),
                     (ropet[0:32, 2, :], cst["rope"][256:288, :]),
                     (g_ffn[:, :], bcast(inp["g_ffn"], DM)), (g_q[:, :], bcast(inp["g_q"], QL)),
                     (g_kv[:, :], bcast(inp["g_kv"], KVL)), (newmask[:, :, :], cst["newmask"]),
                     (newmask_i[:, :], cst["newmask_i"]), (rep[:, :, :], cst["rep"]), (rowsum[:, :, :], cst["rowsum"]),
                     (ones[:, :], cst["ones"]),
                     (w_uq[:, :, :], inp["w_uq"][0].rearrange("(k p) n -> p k n", p=128)),
                     (w_uv[:, :, :], inp["w_uv"][0].rearrange("(k p) h v -> p k (h v)", p=128))]
            early.append((g_fin[:, :], bcast(inp["g_final"], DM)))
            assert 16 * len(early) == CONSTS_IN
            setup = [(relb[:, :], inp["rel_bias"]), (hot_u[:, :], cst["hot"]),
                     (keys_nat[:, :, :], inp["peer_keys"][0].rearrange("h p k d -> k (h p) d")),
                     (uk_nat[:, :, :], inp["w_uk"][0].rearrange("(k p) h n -> p k (h n)", p=128))]
            assert 16 * len(setup) == SETUP_IN
            def chunk(n):
                t, w, c = CHUNKS[n]
                slot, s = wring[n % NW], w_in_slot[n % NW]
                cols = slice(c * CW, min((c + 1) * CW, DIN) if w == "in" else (c + 1) * CW)
                if w == "out":
                    half = NH * VD
                    load(slot[:, 0:4, :], inp["w_out"][0, 0:half, cols].rearrange("(k p) n -> p k n", p=128), s)
                    for g2 in range(KG):
                        load(slot[g2 * 64:g2 * 64 + 64, 4:8, :],
                             inp["w_out"][0, half + g2 * 256:half + (g2 + 1) * 256, cols]
                             .rearrange("(r d) n -> d r n", d=64), s)
                else:
                    load(slot[:, :, 0:cols.stop - cols.start],
                         inp["w_in" if w == "in" else "w_pq"][0, :, cols].rearrange("(k p) n -> p k n", p=128), s)

            def chunk_used(n):
                t, w, c = CHUNKS[n]
                if c % 2 == 0:
                    w_even_used.wait(sp, CHUNKS[n])
                else:
                    ready(sp, ({"in": "z", "out": "wo", "pq": "pq"}[w], c // 2, t))

            page_of = []

            def chunks(t, w, first, last, ids=0):
                for c in range(first, last):
                    n = CHUNKS.index((t, w, c))
                    if n >= NW:
                        chunk_used(n - NW)
                    chunk(n)
                    for i in range(len(page_of), len(page_of) + ids):
                        page_of.append(sp.value_load(page_sb[0:1, i:i + 1], min_val=0,
                                                     max_val=inp["cache_k"].shape[1] - 1))

            def store_rows(t):
                n, zt = P[t], z
                post_ready.wait(sp, t)
                for name, src in (("ckv", ckv_nat[0:n, t, :]), ("kr", kk[0:n, IDX:QKD]), ("k", zt[0:n, O_KB:O_KB + 128]),
                                  ("v", zt[0:n, O_VB:O_VB + 128]), ("ki", kk[0:n, 0:IDX])):
                    o = out[name + "_p"][t * 128:(t + 1) * 128, :] if t < 2 else out[name + "_s"]
                    sp.dma_start(o, src).then_inc(stored_z, 16)

            def pages(which, b):
                moves, arrived = {
                    "index": ([(nat_i[b], inp["cache_kidx"])], idx_in[b]),
                    "lat": ([(nat_c[b % 3], inp["cache_ckv"]), (nat_r[b % 3], inp["cache_krope"])], lat_in[b % 3]),
                    "kv": ([(nat_k[b % 3], inp["cache_k"]), (nat_v[b % 3], inp["cache_v"])], kv_in[b % 3])}[which]

                def move(p, pg):
                    for o, table in moves:
                        tb = table[0]
                        if len(tb.shape) == 4:
                            tb = tb.rearrange("n p g d -> n p (g d)")
                        sp.dma_start(o[:, bass.ds(p, 1), :].rearrange("p a c -> p (a c)"),
                                     tb[bass.ds(pg, 1), :, :].rearrange("a p c -> p (a c)")).then_inc(arrived, 16)

                if b < PRELOADED:
                    for p in range(NPG):
                        move(p, page_of[b * NPG + p])
                else:
                    with sp.Fori(0, NPG) as p:
                        move(p, sp.value_load(page_sb[0:1, bass.ds(p + b * NPG, 1)], min_val=0,
                                              max_val=inp["cache_k"].shape[1] - 1))

            def output(t):
                y_ready.wait(sp, t)
                o = out["y_p"][t * 128:(t + 1) * 128, :] if t < 2 else out["y_s"]
                sp.dma_start(o, xn2[t][0:P[t], :]).then_inc(y_out, 16)

            chunks(0, "in", 0, 2)
            for o, i in setup:
                load(o, i, setup_in)
            for o, i in early:
                load(o, i, consts_in)
            load(page_sb[:, :], inp["page_table"].rearrange("(o b) p -> o (b p)", o=1), page_ids_in)
            load(x[1][:, :], inp["x_prompt"][0, 128:256, :], x_in[1])
            chunks(0, "in", 2, 8)
            for t in (0, 1):
                chunks(t, "out", 0, 2)
                store_rows(t)
                chunks(t, "out", 2, 4)
                if t == 1:
                    sp.wait_ge(page_ids_in, 16)
                chunks(t, "pq", 0, 8, t * PRELOADED)
                chunks(t + 1, "in", 0, 2)
                if t == 1:
                    output(0)
                    load(x[2][0:P[2], :], inp["x_sample"].rearrange("b t d -> (b t) d"), x_in[2])
                chunks(t + 1, "in", 2, 8)
            store_rows(2)
            ready(sp, ("z", 3, 2))
            for b in range(2):
                pages("index", b)
            sp.wait_ge(stored_z, 240)
            ready(sp, ("kv", 2))
            pages("lat", 0)
            for b in range(2, NB):
                pages("index", b)
            for b in range(1, NB):
                if b < 3:
                    ready(sp, ("pi", NB // 2 * b - 1, 1))
                else:
                    lat_used.wait(sp, b - 3)
                pages("lat", b)
            for b in range(NB):
                if b < 3:
                    lat_used.wait(sp, max(a for a in range(NB) if a % 3 == b))
                else:
                    kv_used.wait(sp, b - 3)
                pages("kv", b)
            for c in (1, 0):
                kv_used.wait(sp, max(a for a in range(NB) if a % 3 == c + 1))
                chunk(CHUNKS.index((2, "out", c)))
            chunks(2, "out", 2, 4)
            chunks(2, "pq", 0, 8)
            output(1)
            output(2)
            sp.wait_ge(y_out, 48)
            sp.wait_ge(stored_z, 240)


def shape_constants():
    f = np.float32
    pos = np.concatenate([np.arange(SEQ), np.tile(PAST + np.arange(NT), NB)]).astype(f)
    inv = (f(10000.0) ** (-np.arange(16, dtype=f) / f(16))).astype(f)
    ang = pos[:, None] * inv
    cos, sin = np.cos(ang).astype(f), np.sin(ang).astype(f)
    dist = np.maximum(PAST + NT - 1 - np.arange(GU), 0)
    nf = np.maximum(dist, 1).astype(f)
    large = 16 + (np.log(nf / f(16)) / f(math.log(8.0)) * f(16)).astype(np.int32)
    bucket = np.where(dist < 16, dist, np.minimum(large, REL_B - 1))
    col = np.arange(256)[None, :] - 128
    r = np.arange(32)
    b, t = r // NT, r % NT
    ht = np.arange(32) % NT
    s = np.arange(NB)
    rep = (b[:, None, None] == s[None, :, None]) & (t[:, None, None] == ht[None, None, :])
    newmask = np.where((b[None, None, :] == s[None, :, None]) & (t[None, None, :] <= ht[:, None, None]), 0, NEG)
    newmask_i = np.where((b[None, :] == b[:, None]) & (t[None, :] <= t[:, None]), 0, NEG)
    sel = (np.arange(128)[:, None] % 32) == np.arange(128)[None, :]
    c = {
        "ident": np.eye(128),
        "tri": np.where(col <= np.arange(128)[:, None], 0, NEG),
        "sel": sel, "iota": np.tile(np.arange(16), (128, 1)),
        "rope": np.concatenate([cos, cos, -sin, sin], 1),
        "newmask": newmask, "newmask_i": newmask_i, "rep": rep, "rowsum": rep.transpose(2, 1, 0),
        "ones": np.ones((32, 1)), "hot": np.arange(REL_B)[:, None] == bucket[None, :],
    }
    return {k: np.ascontiguousarray(v, dtype=f) for k, v in c.items()}


INPUTS = ["x_prompt", "x_sample", "cache_ckv", "cache_krope", "cache_k", "cache_v", "cache_kidx", "page_table",
          "rel_bias", "g_attn", "w_in", "g_q", "w_uq", "g_kv", "w_uk", "w_uv", "w_out", "g_ffn", "w_pq", "peer_keys",
          "peer_u", "peer_v", "g_final"]
OUTPUTS = {"y_p": (SEQ, DM), "y_s": (32, DM), "ckv_p": (SEQ, KVL), "kr_p": (SEQ, ROPE), "k_p": (SEQ, 128),
           "v_p": (SEQ, 128), "ki_p": (SEQ, IDX), "ckv_s": (32, KVL), "kr_s": (32, ROPE), "k_s": (32, 128),
           "v_s": (32, 128), "ki_s": (32, IDX)}
SHAPES = [(1, SEQ, DM), (NB, NT, DM), (1, 1, SEQ, KVL), (1, 1, SEQ, ROPE), (1, 1, SEQ, KG, HD), (1, 1, SEQ, KG, HD),
          (1, 1, SEQ, IDX), (1, NB, NT, KVL), (1, NB, NT, ROPE), (1, NB, NT, KG, HD), (1, NB, NT, KG, HD),
          (1, NB, NT, IDX)]


def kernel(**inputs):
    import concourse.bacc as bacc
    from concourse.bass_utils import run_bass_kernel_spmd as run

    nc = bacc.Bacc("TRN2", target_bir_lowering=False, num_devices=1)
    arrays, inp, cst, out = {}, {}, {}, {}
    for name in INPUTS:
        a = np.ascontiguousarray(inputs[name])
        arrays[f"in_{name}"] = a
        inp[name] = nc.dram_tensor(f"in_{name}", a.shape, mybir.dt.from_np(a.dtype), kind="ExternalInput").ap()
    inp["peer_u"], inp["peer_v"] = (inp[n].rearrange("l e d -> (l e) d") for n in ("peer_u", "peer_v"))
    for name, a in shape_constants().items():
        arrays[f"const_{name}"] = a
        cst[name] = nc.dram_tensor(f"const_{name}", a.shape, F32, kind="ExternalInput").ap()
    for name, shape in OUTPUTS.items():
        out[name] = nc.dram_tensor(f"out_{name}", shape, F32, kind="ExternalOutput").ap()
    scr_d = nc.dram_tensor("bias_rows_prompt", (128, NH, WD), F32, kind="Internal").ap()
    scr_s = nc.dram_tensor("bias_rows_sample", (32, WS), F32, kind="Internal").ap()
    build(nc, inp, cst, out, scr_d, scr_s)
    r = run(nc, [arrays], core_ids=[0])
    return tuple(r.results[0][f"out_{n}"].reshape(s) for n, s in zip(OUTPUTS, SHAPES))
```
